# Optimizing a Trainium2 kernel written in Bass

```python
import math
import jax, jax.numpy as jnp
from jax import lax
import numpy as np

D_MODEL = 1024
BATCH = 1
SEQ = 512
DEPTH = 1

NSA_HEADS = 8
NSA_KV_HEADS = 2
HEAD_DIM = 64
NSA_WIDTH = NSA_HEADS * HEAD_DIM
KV_WIDTH = NSA_KV_HEADS * HEAD_DIM
POOL_WIDTH = D_MODEL - NSA_WIDTH
POOL_GROUPS = 4
POOL_GROUP_DIM = POOL_WIDTH // POOL_GROUPS
POOL_WINDOWS = (2, 4, 8, 16)
N_GATES = 3 * NSA_HEADS
IN_WIDTH = NSA_WIDTH + 6 * KV_WIDTH + N_GATES + POOL_WIDTH
CMP_BLOCK = 32
CMP_STRIDE = 16
CMP_HIDDEN = 256
SLC_BLOCK = 64
SLC_COUNT = 16
WINDOW = 512
Q_BLOCK = 128
NEG = -1e30
FORCE = 1e6
N_BUCKETS = 32
MAX_DISTANCE = 128
PEER_HEADS = 8
PEER_KEYS = 128
PEER_EXPERTS = PEER_KEYS * PEER_KEYS
PEER_QDIM = 256
PEER_TOPK = 16
TOKEN_CHUNK = 128
ALPHA = (2 * DEPTH) ** 0.25
BETA = (8 * DEPTH) ** -0.25
LN_EPS = 1e-5

kernel_name = "nsa_pool_peer_hybrid_deepnorm"

def layer_norm(x, g, b):
    xf = x.astype(jnp.float32)
    mu = jnp.mean(xf, axis=-1, keepdims=True)
    var = jnp.mean(jnp.square(xf - mu), axis=-1, keepdims=True)
    return ((xf - mu) * lax.rsqrt(var + LN_EPS)).astype(x.dtype) * g + b

def rel_bucket(dist):
    dist = jnp.maximum(dist, 0)
    max_exact = N_BUCKETS // 2
    large = max_exact + (jnp.log(jnp.maximum(dist, 1).astype(jnp.float32) / max_exact)
                         / math.log(MAX_DISTANCE / max_exact)
                         * (N_BUCKETS - max_exact)).astype(jnp.int32)
    large = jnp.minimum(large, N_BUCKETS - 1)
    return jnp.where(dist < max_exact, dist, large)

def compress(k_raw, pe, w1, w2):
    B, T, G, dh = k_raw.shape
    n_cmp = (T - CMP_BLOCK) // CMP_STRIDE + 1
    idx = jnp.arange(n_cmp)[:, None] * CMP_STRIDE + jnp.arange(CMP_BLOCK)[None, :]
    blocks = k_raw[:, idx] + pe[None, None, :, None, :]
    flat = blocks.transpose(0, 3, 1, 2, 4).reshape(B, G, n_cmp, CMP_BLOCK * dh)
    return jax.nn.gelu(flat @ w1, approximate=False) @ w2

def nsa_attention(q, k_cmp, v_cmp, k_slc, v_slc, k_win, v_win, rel_table):
    B, G, R, T, dh = q.shape
    n_cmp = k_cmp.shape[2]
    n_slc = T // SLC_BLOCK
    k_sel = min(SLC_COUNT, n_slc)
    scale = dh ** -0.5
    cmp_start = jnp.arange(n_cmp) * CMP_STRIDE
    cmp_end = cmp_start + CMP_BLOCK - 1
    slc_start = jnp.arange(n_slc) * SLC_BLOCK
    overlap = ((cmp_start[:, None] <= slc_start[None, :] + SLC_BLOCK - 1)
               & (cmp_end[:, None] >= slc_start[None, :])).astype(jnp.float32)
    pad_k = jnp.pad(k_win, ((0, 0), (0, 0), (WINDOW, 0), (0, 0)))
    pad_v = jnp.pad(v_win, ((0, 0), (0, 0), (WINDOW, 0), (0, 0)))
    tab_g = rel_table.reshape(N_BUCKETS, G, R).transpose(1, 0, 2)
    g_idx = jnp.arange(G)[None, :, None, None]
    b_idx = jnp.arange(B)[:, None, None, None]
    j_idx = jnp.arange(n_slc)
    n_win = Q_BLOCK + WINDOW

    def head_bias(bucket):
        bias = rel_table[bucket]
        return bias.reshape(bucket.shape + (G, R)).transpose(2, 3, 0, 1).astype(jnp.float32)

    def block(qb):
        q0 = qb * Q_BLOCK
        qblk = lax.dynamic_slice_in_dim(q, q0, Q_BLOCK, axis=3)
        t = q0 + jnp.arange(Q_BLOCK)
        s = jnp.einsum('bgrqd,bgnd->bgrqn', qblk, k_cmp).astype(jnp.float32) * scale
        s = s + head_bias(rel_bucket(t[:, None] - cmp_end[None, :]))
        valid = cmp_end[None, :] <= t[:, None]
        p_cmp = jax.nn.softmax(jnp.where(valid, s, NEG), axis=-1) * valid
        o_cmp = jnp.einsum('bgrqn,bgnd->bgrqd', p_cmp.astype(v_cmp.dtype), v_cmp)
        imp = jnp.einsum('bgrqn,nj->bgqj', p_cmp, overlap)
        cur = t // SLC_BLOCK
        forced = (j_idx[None, :] == 0) | (j_idx[None, :] == cur[:, None]) | (j_idx[None, :] == cur[:, None] - 1)
        imp = jnp.where(forced, FORCE, imp)
        imp = jnp.where(slc_start[None, :] <= t[:, None], imp, NEG)
        _, sel = lax.top_k(imp, k_sel)
        pos = (sel[..., None] * SLC_BLOCK + jnp.arange(SLC_BLOCK)).reshape(B, G, Q_BLOCK, k_sel * SLC_BLOCK)
        ks = k_slc[b_idx, g_idx, pos]
        vs = v_slc[b_idx, g_idx, pos]
        s = jnp.einsum('bgrqd,bgqkd->bgrqk', qblk, ks).astype(jnp.float32) * scale
        bias = tab_g[g_idx, rel_bucket(t[None, None, :, None] - pos)]
        s = s + jnp.moveaxis(bias, -1, 2).astype(jnp.float32)
        valid = (pos <= t[None, None, :, None])[:, :, None]
        p_slc = jax.nn.softmax(jnp.where(valid, s, NEG), axis=-1)
        o_slc = jnp.einsum('bgrqk,bgqkd->bgrqd', p_slc.astype(vs.dtype), vs)
        kw = lax.dynamic_slice_in_dim(pad_k, q0, n_win, axis=2)
        vw = lax.dynamic_slice_in_dim(pad_v, q0, n_win, axis=2)
        kpos = q0 - WINDOW + jnp.arange(n_win)
        dist = t[:, None] - kpos[None, :]
        s = jnp.einsum('bgrqd,bgkd->bgrqk', qblk, kw).astype(jnp.float32) * scale
        s = s + head_bias(rel_bucket(dist))
        valid = (dist >= 0) & (dist < WINDOW) & (kpos[None, :] >= 0)
        p_win = jax.nn.softmax(jnp.where(valid, s, NEG), axis=-1)
        o_win = jnp.einsum('bgrqk,bgkd->bgrqd', p_win.astype(vw.dtype), vw)
        return o_cmp, o_slc, o_win

    outs = lax.map(block, jnp.arange(T // Q_BLOCK))
    def to_bthd(o):
        return o.transpose(1, 0, 4, 2, 3, 5).reshape(B, T, G * R, dh)
    return to_bthd(outs[0]), to_bthd(outs[1]), to_bthd(outs[2])

def pool_mixer(z, w, scale):
    B, T, _ = z.shape
    zf = z.astype(jnp.float32).reshape(B, T, POOL_GROUPS, POOL_GROUP_DIM)
    c = jnp.pad(jnp.cumsum(zf, axis=1), ((0, 0), (1, 0), (0, 0), (0, 0)))
    t = jnp.arange(T)
    outs = []
    for gi, win in enumerate(POOL_WINDOWS):
        lo = jnp.maximum(t + 1 - win, 0)
        s = c[:, 1:, gi] - c[:, lo, gi]
        cnt = (t + 1 - lo).astype(jnp.float32)
        outs.append(s / cnt[None, :, None] - zf[:, :, gi])
    y = jnp.stack(outs, axis=2).astype(z.dtype)
    y = jnp.einsum('btgc,gcd->btgd', y, w).reshape(B, T, POOL_WIDTH)
    return y * scale

def peer(h, wq, subkeys, u, v):
    B, T, D = h.shape
    n = B * T
    xf = h.reshape(n, D)
    q = (xf @ wq).reshape(n, PEER_HEADS, 2, PEER_QDIM // 2)
    s1 = jnp.einsum('nhd,kd->nhk', q[:, :, 0], subkeys[0]).astype(jnp.float32)
    s2 = jnp.einsum('nhd,kd->nhk', q[:, :, 1], subkeys[1]).astype(jnp.float32)
    v1, i1 = lax.top_k(s1, PEER_TOPK)
    v2, i2 = lax.top_k(s2, PEER_TOPK)
    cand = (v1[..., :, None] + v2[..., None, :]).reshape(n, PEER_HEADS, PEER_TOPK * PEER_TOPK)
    cand_id = (i1[..., :, None] * PEER_KEYS + i2[..., None, :]).reshape(n, PEER_HEADS, PEER_TOPK * PEER_TOPK)
    sc, ci = lax.top_k(cand, PEER_TOPK)
    eid = jnp.take_along_axis(cand_id, ci, axis=-1)
    gate = jax.nn.softmax(sc, axis=-1)
    nc = n // TOKEN_CHUNK

    def chunk(args):
        xc, ec, gc = args
        act = jax.nn.gelu(jnp.einsum('cd,chkd->chk', xc, u[ec]).astype(jnp.float32), approximate=False)
        return jnp.einsum('chk,chkd->cd', (gc * act).astype(xc.dtype), v[ec])

    out = lax.map(chunk, (xf.reshape(nc, TOKEN_CHUNK, D),
                          eid.reshape(nc, TOKEN_CHUNK, PEER_HEADS, PEER_TOPK),
                          gate.reshape(nc, TOKEN_CHUNK, PEER_HEADS, PEER_TOPK)))
    return out.reshape(B, T, D)

def setup_inputs(seed: int = 0) -> dict:
    key = jax.random.key(seed)
    ks = jax.random.split(key, 24)
    nrm = jax.random.normal
    L, D = DEPTH, D_MODEL
    f = CMP_BLOCK * HEAD_DIM
    return {
        "x": nrm(ks[0], (BATCH, SEQ, D), jnp.float32),
        "w_in": nrm(ks[1], (L, D, IN_WIDTH), jnp.float32) * D ** -0.5,
        "rel_table": nrm(ks[2], (N_BUCKETS, NSA_HEADS), jnp.float32) * 0.5,
        "cmp_pe_k": nrm(ks[3], (L, CMP_BLOCK, HEAD_DIM), jnp.float32) * 0.1,
        "cmp_pe_v": nrm(ks[4], (L, CMP_BLOCK, HEAD_DIM), jnp.float32) * 0.1,
        "cmp_k_w1": nrm(ks[5], (L, f, CMP_HIDDEN), jnp.float32) * f ** -0.5,
        "cmp_k_w2": nrm(ks[6], (L, CMP_HIDDEN, HEAD_DIM), jnp.float32) * CMP_HIDDEN ** -0.5,
        "cmp_v_w1": nrm(ks[7], (L, f, CMP_HIDDEN), jnp.float32) * f ** -0.5,
        "cmp_v_w2": nrm(ks[8], (L, CMP_HIDDEN, HEAD_DIM), jnp.float32) * CMP_HIDDEN ** -0.5,
        "pool_w": nrm(ks[9], (L, POOL_GROUPS, POOL_GROUP_DIM, POOL_GROUP_DIM), jnp.float32) * POOL_GROUP_DIM ** -0.5,
        "pool_scale": 1.0 + 0.02 * nrm(ks[10], (L, POOL_WIDTH), jnp.float32),
        "w_out": nrm(ks[11], (L, D, D), jnp.float32) * (D ** -0.5) * BETA,
        "ln1_g": 1.0 + 0.02 * nrm(ks[12], (L, D), jnp.float32),
        "ln1_b": 0.02 * nrm(ks[13], (L, D), jnp.float32),
        "peer_wq": nrm(ks[14], (L, D, PEER_HEADS * PEER_QDIM), jnp.float32) * D ** -0.5,
        "peer_subkeys": nrm(ks[15], (L, 2, PEER_KEYS, PEER_QDIM // 2), jnp.float32) * (PEER_QDIM // 2) ** -0.5,
        "peer_u": nrm(ks[16], (L, PEER_EXPERTS, D), jnp.float32) * D ** -0.5,
        "peer_v": nrm(ks[17], (L, PEER_EXPERTS, D), jnp.float32) * BETA,
        "ln2_g": 1.0 + 0.02 * nrm(ks[18], (L, D), jnp.float32),
        "ln2_b": 0.02 * nrm(ks[19], (L, D), jnp.float32),
    }

def reference(x, w_in, rel_table, cmp_pe_k, cmp_pe_v, cmp_k_w1, cmp_k_w2, cmp_v_w1, cmp_v_w2,
              pool_w, pool_scale, w_out, ln1_g, ln1_b, peer_wq, peer_subkeys, peer_u, peer_v,
              ln2_g, ln2_b):
    B, T, _ = x.shape
    G, R = NSA_KV_HEADS, NSA_HEADS // NSA_KV_HEADS
    splits = np.cumsum([NSA_WIDTH] + [KV_WIDTH] * 6 + [N_GATES]).tolist()
    h = x
    for l in range(DEPTH):
        proj = h @ w_in[l]
        q, kc, vc, kslc, vslc, kwin, vwin, gates, z = jnp.split(proj, splits, axis=-1)
        q = q.reshape(B, T, G, R, HEAD_DIM).transpose(0, 2, 3, 1, 4)
        kv = lambda a: a.reshape(B, T, G, HEAD_DIM)
        k_cmp = compress(kv(kc), cmp_pe_k[l], cmp_k_w1[l], cmp_k_w2[l])
        v_cmp = compress(kv(vc), cmp_pe_v[l], cmp_v_w1[l], cmp_v_w2[l])
        heads = lambda a: kv(a).transpose(0, 2, 1, 3)
        o_cmp, o_slc, o_win = nsa_attention(q, k_cmp, v_cmp, heads(kslc), heads(vslc),
                                            heads(kwin), heads(vwin), rel_table)
        g = jax.nn.sigmoid(gates.astype(jnp.float32)).astype(x.dtype).reshape(B, T, 3, NSA_HEADS, 1)
        nsa_out = (g[:, :, 0] * o_cmp + g[:, :, 1] * o_slc + g[:, :, 2] * o_win).reshape(B, T, NSA_WIDTH)
        pool_out = pool_mixer(z, pool_w[l], pool_scale[l])
        mix = jnp.concatenate([nsa_out, pool_out], axis=-1) @ w_out[l]
        h = layer_norm(ALPHA * h + mix, ln1_g[l], ln1_b[l])
        ffn = peer(h, peer_wq[l], peer_subkeys[l], peer_u[l], peer_v[l])
        h = layer_norm(ALPHA * h + ffn, ln2_g[l], ln2_b[l])
    return h


_drawn_inputs = setup_inputs


def setup_inputs(seed=0):
    import zlib

    import numpy as np

    out = dict(_drawn_inputs(seed))
    spreads = {}
    factors = {'cmp_pe_k': 16.272, 'pool_scale': 2.671, 'ln2_g': 8.469, 'ln2_b': 8.28}
    for name, (base, spread) in spreads.items():
        noise = np.random.default_rng([zlib.crc32(name.encode()), seed]).standard_normal(out[name].shape)
        drawn = base * np.exp(spread * noise) if base else spread * noise
        out[name] = __import__('jax').numpy.asarray(drawn.astype(out[name].dtype))
    for name, factor in factors.items():
        out[name] = (out[name] * factor).astype(out[name].dtype)
    return out
```

```python
from contextlib import ExitStack

import numpy as np
import concourse.bass as bass
from concourse import mybir

P = 128
T = 512
D = 1024
TT = T // P
KC = D // P
HEADS, GROUPS, DH = 8, 2, 64
PAIRS = HEADS // GROUPS
UNITS = GROUPS * TT
CMP_BLOCK, CMP_STRIDE, CMP_HIDDEN = 32, 16, 256
N_CMP = (T - CMP_BLOCK) // CMP_STRIDE + 1
N_BUCKETS, MAX_DISTANCE = 32, 128
NEG = -1e30
POOL_WINDOWS = (2, 4, 8, 16)
POOL_GROUPS = len(POOL_WINDOWS)
PAD = max(POOL_WINDOWS)
PEER_HEADS, SIDES, TOPK = 8, 2, 16
N_EXP = 128
ALPHA = 2 ** 0.25
LN_EPS = 1e-5
LOWEST, HIGHEST = -3.0e38, 3.0e38

ACT_SCALE = 16.0
W_SCALE = 128.0
GATE_SCALE = 256.0
UNSCALE = 1.0 / (ACT_SCALE * W_SCALE)

FREV = 640
RAW = 3
SPLIT = 3
STEP = 6

F32, F16, U32 = mybir.dt.float32, mybir.dt.float16, mybir.dt.uint32
ALU, ACTF = mybir.AluOpType, mybir.ActivationFunctionType
AX_X = mybir.AxisListType.X

PROJ = ["kc0", "kc1", "vc0", "vc1", "vslc", "vwin", "kslc", "kwin",
        "q0", "q1", "q2", "q3", "z0", "z1", "z2", "z3"]
N_PROJ = len(PROJ)
WOUT_CHUNKS = [4, 5, 6, 7, 0, 1, 2, 3]
FIRST_WOUT = N_PROJ
FIRST_WQ = FIRST_WOUT + KC
FIRST_U = FIRST_WQ + PEER_HEADS * SIDES
FIRST_V = FIRST_U + N_EXP
N_TILES = FIRST_V + N_EXP
Q_STRAIGHT = (PEER_HEADS * SIDES) % STEP
Q_LOOPS = (PEER_HEADS * SIDES) // STEP
V_LOOPS = (N_EXP - RAW) // STEP
AHEAD = SPLIT - 1

SEG_STEPS = 4
SEG = SEG_STEPS * STEP
SEG_TILES = SEG + 1
N_SEG = TT + 1
LAST_U = SEG * N_SEG + TT
TOK_STEP = P // SEG_STEPS
GROUP = 4
STEP_GROUPS = TOK_STEP // GROUP
RING = 4
ROWS_AT = [[0, 1], [2], [3, 4], [5], [6, 7], []]
GROUPS_AT = [[0], [1], [2], [3, 4], [5], [6, 7]]
assert N_EXP - LAST_U > AHEAD

SLC, WIN = range(2)
GATE_CMP = 0


def n_cmp(i):
    return (i + 1) * P // CMP_STRIDE - 1


def layer(nc, x, xT, stream, w_gates, rel, rel_neg, onehot, w1, w2k, w2v, pe_kv, pool_w, pool_scale,
          inv_cnt, row_ok, ln1_g, ln1_b, subkeys, ln2_g, ln2_b, eye, iota_h, iota16, out,
          frev_d, act_d, w_d, res_d):
    ctx, front, first, attn, peer, stage_a, stage_b = (ExitStack() for _ in range(7))

    def sb(name, shape, dt=F32, scope=ctx):
        return scope.enter_context(nc.sbuf_tensor(name, shape, dt))

    def sem(name):
        return ctx.enter_context(nc.semaphore(name))

    raw = sb("raw", [P, RAW, D])
    w_hi = sb("w_hi", [P, SPLIT, D], F16)
    w_lo = sb("w_lo", [P, SPLIT, D], F16)
    a_hi = sb("a_hi", [P, KC, T], F16)
    a_lo = sb("a_lo", [P, KC, T], F16)
    ident = sb("ident", [P, P])
    iota_t = sb("iota_t", [P, P], F16)
    iota16_t = sb("iota16_t", [P, TOPK])
    ln_stats = sb("ln_stats", [P, 2, 6])
    ln_mv = sb("ln_mv", [P, TT, 2])
    ln_rstd = sb("ln_rstd", [P, TT, 2])
    eps_t = sb("eps_t", [P, 1])

    xT_t = sb("xT_t", [P, KC, T], F32, first)
    w1_t = sb("w1_t", [P, 2, CMP_BLOCK // 2, CMP_HIDDEN], F32, first)
    rel_t = sb("rel_t", [N_BUCKETS + 1, HEADS], F32, first)
    onehot_t = sb("onehot_t", [N_BUCKETS + 1, FREV], F32, first)
    frev = sb("frev", [HEADS, FREV], F32, first)
    cmp_in = sb("cmp_in", [P, 2, GROUPS + 1, T // 2], F32, first)
    hid = sb("hid", [P, 2, 2, GROUPS, N_CMP], F32, first)
    hid_b = sb("hid_b", [P, 4], F32, first)
    w2k_t = sb("w2k_t", [P, 2, P], F32, first)
    w2v_t = sb("w2v_t", [P, 2, DH], F32, first)
    w_gates_t = sb("w_gates_t", [P, KC, 3 * HEADS], F32, first)
    first_end = nc.sbuf_base
    first.close()
    neg_x = sb("neg_x", [P, 2, 2, T], F32, attn)
    probs = sb("probs", [P, 2, 2, T], F32, attn)
    probsT = sb("probsT", [P, 2, 2, T], F32, attn)
    neg_max = sb("neg_max", [P, 2, 2], F32, attn)
    row_sum = sb("row_sum", [P, 2, 2], F32, attn)
    row_scale = sb("row_scale", [P, 2, 2, 2], F32, attn)
    neg_xc = sb("neg_xc", [P, TT, 32], F32, attn)
    probs_c = sb("probs_c", [P, TT, 32], F32, attn)
    probsT_c = sb("probsT_c", [N_CMP, GROUPS, T], F32, attn)
    neg_max_c = sb("neg_max_c", [P, TT], F32, attn)
    row_sum_c = sb("row_sum_c", [P, TT], F32, attn)
    row_scale_c = sb("row_scale_c", [P, 2, TT], F32, attn)
    attn_end = nc.sbuf_base
    attn.close()
    sb("front_gap", [P, (max(first_end, attn_end) - nc.sbuf_base + 3) // 4], F32, front)
    bias_all = sb("bias_all", [P, GROUPS, PAIRS, T], F32, front)
    bias_cur = sb("bias_cur", [P, GROUPS, T], F32, front)
    qT = sb("qT", [P, PAIRS, T], F32, front)
    q_cur = sb("q_cur", [P, T], F32, front)
    kT_slc = sb("kT_slc", [P, T], F32, front)
    kT_win = sb("kT_win", [P, T], F32, front)
    v_slc = sb("v_slc", [P, TT, P], F32, front)
    v_win = sb("v_win", [P, TT, P], F32, front)
    gates = sb("gates", [P, TT, 3, HEADS], F32, front)
    kT_cmp = sb("kT_cmp", [P, N_CMP], F32, front)
    v_cmp = sb("v_cmp", [N_CMP, GROUPS, DH], F32, front)
    zp = sb("zp", [P, POOL_GROUPS, PAD + T], F32, front)
    win = sb("win", [P, 2, PAD + T], F32, front)
    inv_t = sb("inv_t", [P, POOL_GROUPS, T], F32, front)
    pool_wt = sb("pool_wt", [P, POOL_GROUPS, P], F32, front)
    pool_sc = sb("pool_sc", [P, POOL_GROUPS], F32, front)
    pool_sc16 = sb("pool_sc16", [P, POOL_GROUPS], F32, front)
    row_ok_t = sb("row_ok_t", [P, 1], F32, front)
    c_hi = sb("c_hi", [P, KC, T], F16, front)
    c_lo = sb("c_lo", [P, KC, T], F16, front)
    lng = sb("lng", [P, D], F32, front)
    lnb = sb("lnb", [P, D], F32, front)
    res = sb("res", [P, TT, D], F32, front)
    front.close()

    w_buf = sb("w_buf", [P, N_EXP, 2, P], F32, peer)
    picks_v = sb("picks_v", [P, TT, PEER_HEADS, SIDES, TOPK], F32, stage_a)
    picks_i = sb("picks_i", [P, TT, PEER_HEADS, SIDES, TOPK], F32, stage_a)
    best_v = sb("best_v", [P, TOPK], F32, stage_a)
    best_i = sb("best_i", [P, TOPK], U32, stage_a)
    best_ab = sb("best_ab", [P, SIDES, TOPK], U32, stage_a)
    eq = sb("eq", [P, SIDES, TOPK, TOPK], F32, stage_a)
    cand, cand_r = eq[:, 0], eq[:, 1]
    score = sb("score", [P, PEER_HEADS, TOPK], F32, stage_a)
    gsum = sb("gsum", [P, 2, PEER_HEADS], F32, stage_a)
    pick3 = sb("pick3", [P, 3, PEER_HEADS, TOPK], F32, stage_a)
    pickT = sb("pickT", [P, 4, P], F32, stage_a)
    gate_h = sb("gate_h", [P, P], F16, stage_a)
    pick_cur = sb("pick_cur", [P, 2, TOK_STEP], F32, stage_a)
    gate_cur = sb("gate_cur", [P, TOK_STEP], F32, stage_a)
    oh2 = sb("oh2", [P, RING, GROUP, P], F16, stage_a)
    eq1 = sb("eq1", [P, RING, GROUP, P], F16, stage_a)
    oh1 = sb("oh1", [P, RING, 2, GROUP, P], F16, stage_a)
    act_out = sb("act_out", [P, RAW, T], F32, stage_a)
    stage_a.close()
    act_in = sb("act_in", [P, RAW, T], F32, stage_b)
    w_in_t = sb("w_in_t", [P, RAW, 2 * P], F32, stage_b)
    g_f = sb("g_f", [P, 2, T], F32, stage_b)
    g_hi = sb("g_hi", [P, 2, T], F16, stage_b)
    g_lo = sb("g_lo", [P, 2, T], F16, stage_b)
    lng2 = sb("lng2", [P, D], F32, stage_b)
    lnb2 = sb("lnb2", [P, D], F32, stage_b)
    stage_b.close()
    peer.close()
    wv = w_buf[:].rearrange("p a b c -> p (a b c)")
    q_s = wv[:, 0:2 * T].rearrange("p (s t) -> p s t", s=2)
    sim = wv[:, 2 * T:4 * T].rearrange("p (s t k) -> p s t k", s=2, t=TT)
    sim_r = wv[:, 4 * T:5 * T].rearrange("p (t k) -> p t k", t=TT)
    subk_t = wv[:, 5 * T:5 * T + 2 * P].rearrange("p (s k) -> p s k", s=2)
    top_v = wv[:, 6 * T:6 * T + TT * TOPK].rearrange("p (t k) -> p t k", t=TT)
    top_i = wv[:, 6 * T + P:6 * T + P + TT * TOPK].bitcast(U32).rearrange("p (t k) -> p t k", t=TT)
    res2 = wv[:, 0:TT * D].rearrange("p (t d) -> p t d", t=TT)

    bank = [ctx.enter_context(nc.psum_tensor(f"bank{i}", [P, 512], F32)) for i in range(8)]
    w_bank = bank[8 - RING:]

    raw_in = [sem(f"raw_in{s}") for s in range(RAW)]
    hi_done, lo_done, tile_used = sem("hi_done"), sem("lo_done"), sem("tile_used")
    x_in = [sem(f"x_in{c}") for c in range(4)]
    x_hi_done, x_lo_done = sem("x_hi_done"), sem("x_lo_done")
    early_in, frev_ps, frev_sb, frev_out, bias_in = (
        sem(s) for s in ("early_in", "frev_ps", "frev_sb", "frev_out", "bias_in"))
    cmp_w_in, pe_in, consts_in, res_in = sem("cmp_w_in"), sem("pe_in"), sem("consts_in"), sem("res_in")
    zeroed = sem("zeroed")
    evac = sem("evac")
    gates_ps, gates_exp, gates_done = sem("gates_ps"), sem("gates_exp"), sem("gates_done")
    hid_ps, hid_b_done, hid_done = sem("hid_ps"), sem("hid_b_done"), sem("hid_done")
    kv_ps, kv_done = sem("kv_ps"), sem("kv_done")
    res_ready, y_done, pool_ps, pool_hi, pool_lo = (
        sem(s) for s in ("res_ready", "y_done", "pool_ps", "pool_hi", "pool_lo"))
    q_ready, bias_ready = sem("q_ready"), sem("bias_ready")
    s_done = sem("s_done")
    x_done = sem("x_done")
    e_done = sem("e_done")
    r_done = sem("r_done")
    t_done = sem("t_done")
    pt_act, pt_dve = sem("pt_act"), sem("pt_dve")
    pv_done = sem("pv_done")
    oT_hi, oT_free = sem("oT_hi"), sem("oT_free")
    mix_done = sem("mix_done")
    ln_var, ln_std, ln_norm, ln_out = sem("ln_var"), sem("ln_std"), sem("ln_norm"), sem("ln_out")
    hT_ps, hT_hi, hT_lo = sem("hT_ps"), sem("hT_hi"), sem("hT_lo")
    res_alpha, res_out, subk_in = sem("res_alpha"), sem("res_out"), sem("subk_in")
    q_done, sim_ps, sim_sb, top_done = sem("q_done"), sem("sim_ps"), sem("sim_sb"), sem("top_done")
    score_done, exp_done, pick_done, pickT_ps, pickT_free = (
        sem(s) for s in ("score_done", "exp_done", "pick_done", "pickT_ps", "pickT_free"))
    eq_done, oh_hi_done, oh_lo_done, pickT_done, wbank_done, wbank_free = (
        sem(s) for s in ("eq_done", "oh_hi_done", "oh_lo_done", "pickT_done", "wbank_done", "wbank_free"))
    w_saved = [sem(f"w_saved{s}") for s in range(2)]
    act_done = sem("act_done")
    act_saved = [sem(f"act_saved{s}") for s in range(RAW)]
    act_back = [sem(f"act_back{s}") for s in range(RAW)]
    g_done, g_hi_done, g_lo_done = sem("g_done"), sem("g_hi_done"), sem("g_lo_done")
    ln2_in, res_back, out_saved = sem("ln2_in"), sem("res_back"), sem("out_saved")

    block = ctx.enter_context(nc.Block())

    def num(b, i):
        return b + STEP * i

    def turn(b, i):
        return b // RAW + (STEP // RAW) * i + 1

    def banks_of(tt):
        return bank[2 * tt], bank[2 * tt + 1]

    @block.sync
    def _(sp):
        def load_tile(b, i=0):
            sp.dma_start(raw[:, b % RAW], stream[num(b, i)]).then_inc(raw_in[b % RAW], 16)

        def next_tile(b, i=0):
            sp.wait_ge(lo_done, num(b, i) + 1)
            load_tile(b + RAW, i)

        sp.dma_start(rel_t[0:N_BUCKETS, :], rel).then_inc(early_in, 16)
        sp.dma_start(rel_t[N_BUCKETS:N_BUCKETS + 1, :], rel_neg).then_inc(early_in, 16)
        sp.dma_start(onehot_t[:], onehot).then_inc(early_in, 16)
        for c in range(4):
            sp.dma_start(xT_t[:, 2 * c:2 * c + 2], xT[:, 2 * c:2 * c + 2]).then_inc(x_in[c], 16)
            if c < RAW:
                load_tile(c)
        sp.dma_start(w_gates_t[:], w_gates).then_inc(consts_in, 16)
        for dst, src in ((ident, eye), (row_ok_t, row_ok), (inv_t, inv_cnt), (pool_wt, pool_w),
                         (pool_sc, pool_scale), (iota_t, iota_h), (iota16_t, iota16)):
            sp.dma_start(dst[:], src).then_inc(consts_in, 16)
        sp.wait_ge(frev_sb, 1)
        sp.dma_start(frev_d, frev[:].unsqueeze(1).to_broadcast([HEADS, P, FREV])).then_inc(frev_out, 16)
        next_tile(0)
        sp.dma_start(w1_t[:, 0], w1[0]).then_inc(cmp_w_in, 16)
        sp.wait_ge(zeroed, 1)
        sp.dma_start(cmp_in[:, :, GROUPS, 0:CMP_BLOCK // 2], pe_kv).then_inc(pe_in, 16)
        next_tile(1)
        sp.dma_start(w1_t[:, 1], w1[1]).then_inc(cmp_w_in, 16)
        sp.dma_start(w2k_t[:], w2k).then_inc(cmp_w_in, 16)
        sp.dma_start(w2v_t[:], w2v).then_inc(cmp_w_in, 16)
        next_tile(2)
        sp.wait_ge(frev_out, 16)
        skew = bass.AP(frev_d.tensor, P - 1, [[FREV - 1, P], [P * FREV, HEADS], [1, T]])
        sp.dma_start(bias_all[:].rearrange("p g j t -> p (g j) t"), skew).then_inc(bias_in, 16)
        for b in range(3, N_PROJ):
            next_tile(b)
        sp.dma_start(res[:], x.rearrange("(t p) d -> p t d", p=P)).then_inc(res_in, 16)
        sp.dma_start(lng[:], ln1_g).then_inc(res_in, 16)
        sp.dma_start(lnb[:], ln1_b).then_inc(res_in, 16)
        for b in range(FIRST_WOUT, FIRST_WQ):
            next_tile(b)
        sp.wait_ge(res_alpha, TT)
        sp.dma_start(res_d.rearrange("(t p) d -> p t d", p=P), res[:]).then_inc(res_out, 16)
        sp.wait_ge(hT_lo, TT)
        sp.dma_start(subk_t, subkeys).then_inc(subk_in, 16)
        for b in range(FIRST_WQ, FIRST_WQ + Q_STRAIGHT):
            next_tile(b)
        with sp.Fori(0, Q_LOOPS) as i:
            for k in range(STEP):
                next_tile(FIRST_WQ + Q_STRAIGHT + k, i)

        def save_act(m, i=0):
            sp.wait_ge(act_done, num(m, i) + 1)
            sp.dma_start(act_d[num(m, i)], act_out[:, m % RAW]).then_inc(act_saved[m % RAW], 16)

        def save_w(tt, st, quarter):
            i1 = (N_EXP // SEG_STEPS) * st + 8 * quarter
            sp.dma_start(w_d[:, bass.ds(i1, 8), tt * P:(tt + 1) * P],
                         w_buf[:, bass.ds(i1, 8), tt % 2, :]).then_inc(w_saved[tt], 16)

        def step(seg, st, m0=0):
            base = seg * SEG_TILES
            for k in range(STEP):
                next_tile(FIRST_U + base + k, st)
                if base + k > 0:
                    save_act(base + k - 1, st)
                elif m0:
                    save_act(base + k - 1, st)
                if seg in (2, 3) and k in (1, 2, 4, 5):
                    save_w(seg - 2, st, (1, 2, 4, 5).index(k))

        def load_g(m, i=0):
            s = m % RAW
            sp.dma_start(act_in[:, s], act_d[num(m, i)]).then_inc(act_back[s], 16)
            sp.dma_start(w_in_t[:, s], w_d[:, num(m, i)]).then_inc(act_back[s], 16)

        for seg in range(N_SEG):
            if seg == 0:
                step(0, 0)
                with sp.Fori(1, SEG_STEPS) as st:
                    step(0, st, 1)
            else:
                if seg in (2, 3):
                    sp.wait_ge(wbank_free, RING + (seg - 1) * (P // GROUP))
                with sp.Fori(0, SEG_STEPS) as st:
                    step(seg, st)
            if seg < N_SEG - 1:
                m = seg * SEG_TILES + SEG
                next_tile(FIRST_U + m)
                save_act(m - 1)
            if seg == TT - 1:
                for s in range(2):
                    sp.wait_ge(w_saved[s], 16 * 16)
                for s in range(RAW):
                    sp.wait_ge(act_saved[s], 16 * ((m - s + RAW - 1) // RAW))
                sp.wait_ge(pickT_done, TT)
                for g in range(RAW):
                    load_g(g)
        for m in range(LAST_U, N_EXP):
            next_tile(FIRST_U + m)
            save_act(m - 1)
            if m == LAST_U:
                sp.wait_ge(wbank_free, RING + T // GROUP)
                sp.dma_start(lng2[:], ln2_g).then_inc(ln2_in, 16)
                sp.dma_start(lnb2[:], ln2_b).then_inc(ln2_in, 16)
        save_act(N_EXP - 1)
        for s in range(RAW):
            sp.wait_ge(act_saved[s], 16 * ((N_EXP - s + RAW - 1) // RAW))

        def v_body(m, i=0):
            next_tile(FIRST_V + m, i)
            sp.wait_ge(g_done, num(m, i) + 1)
            load_g(m + RAW, i)

        with sp.Fori(0, V_LOOPS) as i:
            for k in range(STEP):
                v_body(k, i)
        for m in range(V_LOOPS * STEP, N_EXP - RAW):
            v_body(m)
        sp.wait_ge(g_done, N_EXP)
        sp.dma_start(res2, res_d.rearrange("(t p) d -> p t d", p=P)).then_inc(res_back, 16)
        for tt in range(TT):
            sp.wait_ge(ln_out, TT + tt + 1)
            sp.dma_start(out[tt * P:(tt + 1) * P, :], res2[:, tt]).then_inc(out_saved, 16)
        sp.wait_ge(out_saved, 16 * TT)

    @block.scalar
    def _(act):
        def hi(b, i=0):
            act.wait_ge(raw_in[b % RAW], 16 * turn(b, i))
            if b >= SPLIT:
                act.wait_ge(tile_used, num(b, i) - SPLIT + 1)
            nc.scalar.activation(w_hi[:, b % SPLIT], raw[:, b % RAW], ACTF.Copy,
                                 scale=W_SCALE).then_inc(hi_done, 1)

        for c in range(4):
            act.wait_ge(x_in[c], 16)
            nc.scalar.activation(a_hi[:, 2 * c:2 * c + 2], xT_t[:, 2 * c:2 * c + 2], ACTF.Copy,
                                 scale=ACT_SCALE).then_inc(x_hi_done, 1)
            if c < AHEAD:
                hi(c)

        def copy_out(b):
            name, ps = PROJ[b], bank[b % 2]
            act.wait_ge(tile_used, b + 1)
            if name[:2] in ("kc", "vc"):
                kv, g = int(name[0] == "v"), int(name[2])
                two = ps[:].rearrange("p (t o) -> p t o", o=2)
                nc.scalar.activation(cmp_in[0:DH, kv, g, :], two[0:DH, :, 0], ACTF.Copy, scale=UNSCALE)
                done = nc.scalar.activation(cmp_in[DH:P, kv, g, :], two[DH:P, :, 1], ACTF.Copy,
                                            scale=UNSCALE)
            elif name[0] == "z":
                done = nc.scalar.activation(zp[:, int(name[1]), PAD:], ps[:], ACTF.Copy, scale=UNSCALE)
            elif name[0] == "q":
                done = nc.scalar.activation(qT[:, int(name[1]), :], ps[:], ACTF.Copy,
                                            scale=UNSCALE * DH ** -0.5)
            else:
                dst = {"kslc": kT_slc[:], "kwin": kT_win[:],
                       "vslc": v_slc[:].rearrange("p t d -> p (t d)"),
                       "vwin": v_win[:].rearrange("p t d -> p (t d)")}[name]
                done = nc.scalar.activation(dst, ps[:], ACTF.Copy, scale=UNSCALE)
            done.then_inc(evac, 1)

        for b in range(N_PROJ):
            hi(b + AHEAD)
            copy_out(b)
            if b == 8:
                act.wait_ge(gates_ps, 1)
                nc.scalar.activation(gates[:].rearrange("p t b h -> p t (b h)"),
                                     bank[4][:, 0:TT * 3 * HEADS].rearrange("p (t n) -> p t n", t=TT),
                                     ACTF.Exp, scale=-1.0).then_inc(gates_exp, 1)
                act.wait_ge(hid_b_done, 1)
                for kv in range(2):
                    for mh in range(2):
                        o = (2 * kv + mh) * 3 * N_CMP
                        done = nc.scalar.activation(
                            hid[:, kv, mh].rearrange("p g n -> p (g n)"), bank[2][:, o:o + 2 * N_CMP],
                            ACTF.Gelu, bias=hid_b[:, 2 * kv + mh:2 * kv + mh + 1])
                done.then_inc(hid_done, 1)
            if b == 10:
                act.wait_ge(kv_ps, 1)
                nc.scalar.copy(kT_cmp[0:DH, :], bank[3][0:DH, 0:N_CMP])
                nc.scalar.copy(kT_cmp[DH:P, :], bank[3][DH:P, N_CMP:2 * N_CMP])
                nc.scalar.copy(v_cmp[:].rearrange("n g d -> n (g d)"),
                               bank[3][0:N_CMP, 64:64 + GROUPS * DH]).then_inc(kv_done, 1)

        def exps(u, j):
            i, par = u % TT, u % 2
            act.wait_ge(x_done, UNITS * j + u + 1)
            if u >= 2:
                act.wait_ge(t_done, UNITS * j + u - 1)
            if i == 0:
                for c in range(TT):
                    nc.scalar.activation(probs_c[:, c, 0:n_cmp(c)], neg_xc[:, c, 0:n_cmp(c)], ACTF.Exp,
                                         scale=-1.0, bias=neg_max_c[:, c:c + 1],
                                         accum_out=row_sum_c[:, c:c + 1])
            n = (i + 1) * P
            for br in (SLC, WIN):
                done = nc.scalar.activation(probs[:, par, br, 0:n], neg_x[:, par, br, 0:n], ACTF.Exp,
                                            scale=-1.0, bias=neg_max[:, par, br:br + 1],
                                            accum_out=row_sum[:, par, br:br + 1])
            done.then_inc(e_done, 1)

        def copy_pT(u, j):
            i, par = u % TT, u % 2
            act.wait_ge(t_done, UNITS * j + u + 1)
            if u >= 2:
                act.wait_ge(pv_done, UNITS * j + u - 1)
            nc.scalar.copy(probsT[:, par, SLC, 0:(i + 1) * P], bank[5][:, 0:(i + 1) * P])
            nc.scalar.copy(probsT[:, par, WIN, 0:(i + 1) * P],
                           bank[6][:, 0:(i + 1) * P]).then_inc(pt_act, 1)

        with act.Fori(0, PAIRS) as j:
            for u in range(UNITS + 1):
                if u < UNITS:
                    exps(u, j)
                if u >= 1:
                    copy_pT(u - 1, j)
            act.wait_ge(pv_done, UNITS * j + UNITS)
            nc.scalar.activation(c_hi[:, j, :], bank[7][:], ACTF.Copy, scale=ACT_SCALE).then_inc(oT_hi, 1)

        for g in range(POOL_GROUPS):
            act.wait_ge(pool_ps, g + 1)
            nc.scalar.activation(c_hi[:, PAIRS + g, :], bank[g][:], ACTF.Copy,
                                 scale=pool_sc16[:, g:g + 1]).then_inc(pool_hi, 1)
        for b in range(FIRST_WOUT, FIRST_WQ):
            hi(b + AHEAD)

        def ln_sqrt(tt, n):
            act.wait_ge(ln_var, n + 1)
            nc.scalar.activation(ln_rstd[:, tt, 0:1], ln_mv[:, tt, 1:2], ACTF.Sqrt,
                                 bias=eps_t[:]).then_inc(ln_std, 1)

        for s in range(TT + 2):
            if s < TT:
                ln_sqrt(s, s)
            if s >= 2:
                tt = s - 2
                act.wait_ge(hT_ps, tt + 1)
                for half, ps in enumerate(banks_of(tt)):
                    done = nc.scalar.activation(
                        a_hi[:, 4 * half:4 * half + 4, tt * P:(tt + 1) * P],
                        ps[:].rearrange("p (c t) -> p c t", c=4), ACTF.Copy, scale=ACT_SCALE)
                done.then_inc(hT_hi, 1)
                nc.scalar.mul(res[:, tt], res[:, tt], ALPHA).then_inc(res_alpha, 1)

        def query(hs, i=0):
            b = FIRST_WQ + hs
            hi(b + AHEAD, i)
            act.wait_ge(tile_used, num(b, i) + 1)
            if hs >= 2:
                act.wait_ge(sim_ps, num(hs, i) - 1)
            nc.scalar.activation(q_s[:, hs % 2], bank[b % 2][:], ACTF.Copy,
                                 scale=UNSCALE).then_inc(q_done, 1)
            if hs >= 1:
                copy_sim(hs - 1, i)

        def copy_sim(hs, i=0):
            act.wait_ge(sim_ps, num(hs, i) + 1)
            if hs >= 2:
                act.wait_ge(top_done, num(hs, i) - 1)
            nc.scalar.copy(sim[:, hs % 2].rearrange("p t k -> p (t k)"),
                           bank[5 + hs % 2][:]).then_inc(sim_sb, 1)

        for hs in range(Q_STRAIGHT):
            query(hs)
        with act.Fori(0, Q_LOOPS) as i:
            for k in range(STEP):
                query(Q_STRAIGHT + k, i)
        copy_sim(PEER_HEADS * SIDES - 1)

        act.wait_ge(res_out, 16)

        def gelu(m, i=0, later=False):
            b = FIRST_U + m
            act.wait_ge(tile_used, num(b, i) + 1)
            if m >= RAW or later:
                act.wait_ge(act_saved[m % RAW], 16 * (turn(m, i) - 1))
            nc.scalar.activation(act_out[:, m % RAW], bank[b % 2][:], ACTF.Gelu,
                                 scale=UNSCALE).then_inc(act_done, 1)

        def copy_w(tt, st, q):
            n = tt * (P // GROUP) + STEP_GROUPS * st + q
            act.wait_ge(wbank_done, n + RING + 1)
            nc.scalar.activation(w_buf[:, :, tt % 2, bass.ds(TOK_STEP * st + GROUP * q, GROUP)],
                                 w_bank[q % RING][:].rearrange("p (t i) -> p i t", t=GROUP), ACTF.Copy,
                                 scale=1.0 / GATE_SCALE).then_inc(wbank_free, 1)

        def gate_high(tt, st, q):
            act.wait_ge(eq_done, tt * (P // GROUP) + STEP_GROUPS * st + q + 1)
            for t in range(GROUP):
                c = GROUP * q + t
                done = nc.scalar.activation(oh1[:, q % RING, 0, t], eq1[:, q % RING, t], ACTF.Copy,
                                            scale=gate_cur[:, c:c + 1])
            done.then_inc(oh_hi_done, 1)

        def step(seg, st, later=False):
            for k in range(STEP):
                hi(FIRST_U + seg * SEG_TILES + k + AHEAD, st)
                if seg >= 1:
                    if k == 0:
                        act.wait_ge(pickT_done, seg)
                        nc.scalar.copy(gate_cur[:], pickT[:, 2, bass.ds(TOK_STEP * st, TOK_STEP)])
                        act.drain()
                    for q in GROUPS_AT[k]:
                        gate_high(seg - 1, st, q)
                gelu(seg * SEG_TILES + k, st, later)
                if seg >= 1:
                    for q in GROUPS_AT[k]:
                        copy_w(seg - 1, st, q)

        act.sem_inc(wbank_free, RING)
        for seg in range(N_SEG):
            if seg == 0:
                step(0, 0)
                with act.Fori(1, SEG_STEPS) as st:
                    step(0, st, True)
            else:
                if seg >= 3:
                    act.wait_ge(w_saved[seg - 3], 16 * 16)
                with act.Fori(0, SEG_STEPS) as st:
                    step(seg, st)
            if seg < N_SEG - 1:
                hi(FIRST_U + seg * SEG_TILES + SEG + AHEAD)
                act.wait_ge(score_done, seg + 1)
                nc.scalar.activation(score[:], score[:], ACTF.Exp).then_inc(exp_done, 1)
                gelu(seg * SEG_TILES + SEG)

        def g_high(m, i=0):
            act.wait_ge(g_done, num(m, i) + 1)
            if m >= 1:
                act.wait_ge(tile_used, num(FIRST_V + m, i) - 1)
            nc.scalar.activation(g_hi[:, m % 2], g_f[:, m % 2], ACTF.Copy,
                                 scale=ACT_SCALE).then_inc(g_hi_done, 1)

        for m in range(LAST_U, N_EXP):
            hi(FIRST_U + m + AHEAD)
            gelu(m)
            if m == N_EXP - 2:
                g_high(0)

        def v_body(m, i=0):
            if m + AHEAD < N_EXP:
                hi(FIRST_V + m + AHEAD, i)
            g_high(m + 1, i)

        with act.Fori(0, V_LOOPS) as i:
            for k in range(STEP):
                v_body(k, i)
        for m in range(V_LOOPS * STEP, N_EXP - 1):
            v_body(m)
        for tt in range(TT):
            ln_sqrt(tt, TT + tt)

    @block.vector
    def _(dve):
        def lo(b, i=0):
            dve.wait_ge(hi_done, num(b, i) + 1)
            nc.vector.scalar_tensor_tensor(
                out=w_lo[:, b % SPLIT], in0=raw[:, b % RAW], scalar=W_SCALE, in1=w_hi[:, b % SPLIT],
                op0=ALU.mult, op1=ALU.subtract).then_inc(lo_done, 1)

        def low_of(dst, src, high, scale=ACT_SCALE):
            return nc.vector.scalar_tensor_tensor(out=dst, in0=src, scalar=scale, in1=high,
                                                  op0=ALU.mult, op1=ALU.subtract)

        nc.vector.memset(eps_t[:], LN_EPS)
        for c in range(4):
            dve.wait_ge(x_hi_done, c + 1)
            low_of(a_lo[:, 2 * c:2 * c + 2], xT_t[:, 2 * c:2 * c + 2],
                   a_hi[:, 2 * c:2 * c + 2]).then_inc(x_lo_done, 1)
            if c < AHEAD:
                lo(c)
            if c == 0:
                dve.wait_ge(frev_ps, 1)
                nc.vector.tensor_copy(frev[:, 0:FREV // 2], bank[5][0:HEADS, 0:FREV // 2])
                nc.vector.tensor_copy(frev[:, FREV // 2:], bank[6][0:HEADS, 0:FREV // 2]).then_inc(frev_sb, 1)
        for b in range(N_PROJ):
            lo(b + AHEAD)
            if b == 7:
                dve.wait_ge(consts_in, 16 * 8)
                nc.vector.tensor_scalar(pool_sc16[:], pool_sc[:], ACT_SCALE, None, ALU.mult)
                dve.wait_ge(hid_ps, 1)
                ps = bank[2][:, 0:12 * N_CMP].rearrange("p (a g n) -> p a g n", a=4, g=3)
                nc.vector.tensor_copy(hid_b[:], ps[:, :, GROUPS, 0]).then_inc(hid_b_done, 1)
            if b == 9:
                gv = gates[:].rearrange("p t b h -> p (t b h)")
                dve.wait_ge(gates_exp, 1)
                nc.vector.tensor_scalar(gv, gv, 1.0, None, ALU.add)
                dve.drain()
                nc.vector.reciprocal(gv, gv)
                dve.drain()
                nc.vector.tensor_scalar(gates[:, 0, GATE_CMP], gates[:, 0, GATE_CMP], row_ok_t[:], None, ALU.mult)
                dve.drain()

        def bias_max(u, j):
            g, i, par = u // TT, u % TT, u % 2
            if i == 0:
                dve.wait_ge(bias_ready, GROUPS * j + g + 1)
            dve.wait_ge(s_done, UNITS * j + u + 1)
            if u >= 2:
                dve.wait_ge(e_done, UNITS * j + u - 1)
            dve.nop(nofuse=True)
            first_c = T - (i + 1) * P
            if i == 0:
                for c in range(TT):
                    c0 = T - (c + 1) * P + CMP_BLOCK - 1
                    nc.vector.tensor_tensor_reduce(
                        out=neg_xc[:, c, 0:n_cmp(c)], in0=bank[4][:, 32 * c:32 * c + n_cmp(c)],
                        in1=bias_cur[:, g, c0:c0 + CMP_STRIDE * (n_cmp(c) - 1) + 1:CMP_STRIDE],
                        scale=-1.0, scalar=HIGHEST, op0=ALU.add, op1=ALU.min,
                        accum_out=neg_max_c[:, c:c + 1])
            for br in (SLC, WIN):
                done = nc.vector.tensor_tensor_reduce(
                    out=neg_x[:, par, br, 0:(i + 1) * P], in0=bank[2 * br + par][:, 0:(i + 1) * P],
                    in1=bias_cur[:, g, first_c:], scale=-1.0, scalar=HIGHEST,
                    op0=ALU.add, op1=ALU.min, accum_out=neg_max[:, par, br:br + 1])
            done.then_inc(x_done, 1)

        def rescale(u, j):
            g, i, par = u // TT, u % TT, u % 2
            head = bass.ds(j + PAIRS * g, 1)
            dve.wait_ge(e_done, UNITS * j + u + 1)
            dve.nop(nofuse=True)
            if i == 0:
                nc.vector.reciprocal(row_scale_c[:, 0], row_sum_c[:])
            nc.vector.reciprocal(row_scale[:, par, 0], row_sum[:, par])
            dve.drain()
            if i == 0:
                nc.vector.tensor_tensor(row_scale_c[:, 1], row_scale_c[:, 0],
                                        gates[:, :, GATE_CMP, head].rearrange("p t o -> p (t o)"), ALU.mult)
            nc.vector.tensor_tensor(row_scale[:, par, 1], row_scale[:, par, 0],
                                    gates[:, i, GATE_CMP + 1:, head].rearrange("p b o -> p (b o)"),
                                    ALU.mult)
            dve.drain()
            if i == 0:
                for c in range(TT):
                    nc.vector.tensor_scalar(probs_c[:, c, 0:n_cmp(c)], probs_c[:, c, 0:n_cmp(c)],
                                            row_scale_c[:, 1, c:c + 1], None, ALU.mult)
            n = (i + 1) * P
            for br in (SLC, WIN):
                done = nc.vector.tensor_scalar(probs[:, par, br, 0:n], probs[:, par, br, 0:n],
                                               row_scale[:, par, 1, br:br + 1], None, ALU.mult)
            done.then_inc(r_done, 1)

        def copy_pT_cmp(g, j):
            dve.wait_ge(t_done, UNITS * j + TT * g + 1)
            nc.vector.tensor_copy(probsT_c[:, g, :], bank[4][0:N_CMP, :]).then_inc(pt_dve, 1)

        dve.wait_ge(kv_done, 1)
        nc.vector.memset(probs_c[:], 0.0)
        dve.drain()
        dve.sem_inc(oT_free, 1)
        with dve.Fori(0, PAIRS) as j:
            for u in range(UNITS + 1):
                if u < UNITS:
                    bias_max(u, j)
                if u >= 1:
                    rescale(u - 1, j)
                    if (u - 1) % TT == 0:
                        copy_pT_cmp((u - 1) // TT, j)
            dve.wait_ge(oT_hi, j + 1)
            low_of(c_lo[:, j, :], bank[7][:], c_hi[:, j, :]).then_inc(oT_free, 1)

        for g in range(POOL_GROUPS):
            dve.wait_ge(pool_hi, g + 1)
            low_of(c_lo[:, PAIRS + g, :], bank[g][:], c_hi[:, PAIRS + g, :],
                   pool_sc16[:, g:g + 1]).then_inc(pool_lo, 1)
        for b in range(FIRST_WOUT, FIRST_WQ):
            lo(b + AHEAD)

        def ln_moments(r, tt, n, unscale):
            dve.wait_ge(mix_done, n + 1)
            for half, ps in enumerate(banks_of(tt)):
                h = slice(half * T, (half + 1) * T)
                nc.vector.scalar_tensor_tensor(out=r[:, tt, h], in0=ps[:], scalar=unscale, in1=r[:, tt, h],
                                               op0=ALU.mult, op1=ALU.add)
            dve.drain()
            for half in range(2):
                nc.vector.bn_stats(ln_stats[:, half], r[:, tt, half * T:(half + 1) * T])
            dve.drain()
            nc.vector.bn_aggr(ln_mv[:, tt], ln_stats[:].rearrange("p a b -> p (a b)")).then_inc(ln_var, 1)

        def ln_normal(r, tt, n):
            dve.wait_ge(ln_std, n + 1)
            nc.vector.reciprocal(ln_rstd[:, tt, 1:2], ln_rstd[:, tt, 0:1])
            dve.drain()
            nc.vector.tensor_scalar(r[:, tt], r[:, tt], ln_mv[:, tt, 0:1], ln_rstd[:, tt, 1:2],
                                    ALU.subtract, ALU.mult).then_inc(ln_norm, 1)

        dve.wait_ge(res_ready, 1)
        for s in range(TT + 2):
            if s < TT:
                ln_moments(res, s, s, UNSCALE)
            if 1 <= s <= TT:
                ln_normal(res, s - 1, s - 1)
            if s >= 2:
                tt = s - 2
                dve.wait_ge(hT_hi, tt + 1)
                for half, ps in enumerate(banks_of(tt)):
                    at = (slice(None), slice(4 * half, 4 * half + 4), slice(tt * P, (tt + 1) * P))
                    done = low_of(a_lo[at], ps[:].rearrange("p (c t) -> p c t", c=4), a_hi[at])
                done.then_inc(hT_lo, 1)

        def top_keys(hs, i=0):
            s = sim[:, hs % 2]
            dve.wait_ge(sim_sb, num(hs, i) + 1)
            dve.nop(nofuse=True)
            for tt in range(TT):
                nc.vector.max(top_v[:, tt, 0:8], s[:, tt])
            dve.drain()
            for tt in range(TT):
                nc.vector.match_replace(sim_r[:, tt], in_to_replace=top_v[:, tt, 0:8], in_values=s[:, tt],
                                        imm_value=LOWEST)
            dve.drain()
            for tt in range(TT):
                nc.vector.max(top_v[:, tt, 8:16], sim_r[:, tt])
                nc.vector.max_index(top_i[:, tt, 0:8], top_v[:, tt, 0:8], s[:, tt])
            dve.drain()
            for tt in range(TT):
                nc.vector.max_index(top_i[:, tt, 8:16], top_v[:, tt, 8:16], sim_r[:, tt])
            dve.drain()
            head = hs // SIDES + (STEP // SIDES) * i
            for dst, src in ((picks_v, top_v), (picks_i, top_i)):
                done = nc.vector.tensor_copy(
                    dst[:, :, bass.ds(head, 1), hs % SIDES, :].rearrange("p t o k -> p t (o k)"), src)
            done.then_inc(top_done, 1)
            dve.drain()

        def query(hs, i=0):
            lo(FIRST_WQ + hs + AHEAD, i)
            if hs >= 1:
                top_keys(hs - 1, i)

        for hs in range(Q_STRAIGHT):
            query(hs)
        with dve.Fori(0, Q_LOOPS) as i:
            for k in range(STEP):
                query(Q_STRAIGHT + k, i)
        top_keys(PEER_HEADS * SIDES - 1)

        def best_pairs(tt, st, sub):
            h = bass.ds(2 * st + sub, 1)
            a = picks_v[:, tt, h, 0, :].rearrange("p o k -> p (o k)").unsqueeze(2).to_broadcast([P, TOPK, TOPK])
            b = picks_v[:, tt, h, 1, :].to_broadcast([P, TOPK, TOPK])
            nc.vector.tensor_tensor(cand, a, b, ALU.add)
            dve.drain()
            c, r = (t.rearrange("p a b -> p (a b)") for t in (cand, cand_r))
            nc.vector.max(best_v[:, 0:8], c)
            dve.drain()
            nc.vector.match_replace(r, in_to_replace=best_v[:, 0:8], in_values=c, imm_value=LOWEST)
            dve.drain()
            nc.vector.max(best_v[:, 8:16], r)
            nc.vector.max_index(best_i[:, 0:8], best_v[:, 0:8], c)
            dve.drain()
            nc.vector.max_index(best_i[:, 8:16], best_v[:, 8:16], r)
            nc.vector.tensor_scalar(score[:, h, :].rearrange("p o k -> p (o k)"), best_v[:], best_v[:, 0:1],
                                    None, ALU.subtract)
            dve.drain()

        def expert_ids(tt, st, sub):
            h = bass.ds(2 * st + sub, 1)
            nc.vector.tensor_scalar(best_ab[:, 0], best_i[:], 4, None, ALU.logical_shift_right)
            nc.vector.tensor_scalar(best_ab[:, 1], best_i[:], 15, None, ALU.bitwise_and)
            dve.drain()
            sides = [P, SIDES * TOPK, TOPK]
            nc.vector.tensor_tensor(eq[:].rearrange("p s k a -> p (s k) a"),
                                    best_ab[:].rearrange("p s k -> p (s k)").unsqueeze(2).to_broadcast(sides),
                                    iota16_t[:].unsqueeze(1).to_broadcast(sides), ALU.is_equal)
            dve.drain()
            ids = picks_i[:, tt, h].rearrange("p o s k -> p (o s) k").unsqueeze(2)
            nc.vector.tensor_tensor(eq[:], eq[:], ids.to_broadcast([P, SIDES, TOPK, TOPK]), ALU.mult)
            dve.drain()
            nc.vector.tensor_reduce(pick3[:, 0:2, h, :].rearrange("p s o k -> p s (o k)"), eq[:],
                                    AX_X, ALU.add)
            dve.drain()

        def one_hots(tt, st, q):
            dve.wait_ge(wbank_done, tt * (P // GROUP) + STEP_GROUPS * st + q + 1)
            for t in range(GROUP):
                c = GROUP * q + t
                nc.vector.tensor_scalar(eq1[:, q % RING, t], iota_t[:], pick_cur[:, 0, c:c + 1], None,
                                        ALU.is_equal)
                done = nc.vector.tensor_scalar(oh2[:, q % RING, t], iota_t[:], pick_cur[:, 1, c:c + 1], None,
                                               ALU.is_equal)
            done.then_inc(eq_done, 1)

        def step(seg, st):
            for k in range(STEP):
                if seg >= 1:
                    if k == 0:
                        dve.drain()
                        nc.vector.tensor_copy(pick_cur[:], pickT[:, 0:2, bass.ds(TOK_STEP * st, TOK_STEP)])
                        dve.drain()
                    for q in ROWS_AT[k]:
                        one_hots(seg - 1, st, q)
                if seg < TT:
                    if k == 1:
                        best_pairs(seg, st, 0)
                    if k == 3:
                        expert_ids(seg, st, 0)
                    if k == 5:
                        best_pairs(seg, st, 1)
                        expert_ids(seg, st, 1)
                lo(FIRST_U + seg * SEG_TILES + k + AHEAD, st)

        dve.wait_ge(res_out, 16)
        for seg in range(N_SEG):
            with dve.Fori(0, SEG_STEPS) as st:
                step(seg, st)
            if seg < N_SEG - 1:
                dve.drain().then_inc(score_done, 1)
                lo(FIRST_U + seg * SEG_TILES + SEG + AHEAD)
                dve.wait_ge(exp_done, seg + 1)
                nc.vector.tensor_reduce(gsum[:, 0], score[:], AX_X, ALU.add)
                dve.drain()
                nc.vector.reciprocal(gsum[:, 1], gsum[:, 0])
                dve.drain()
                nc.vector.scalar_tensor_tensor(
                    out=pick3[:, 2], in0=score[:], scalar=GATE_SCALE,
                    in1=gsum[:, 1].unsqueeze(2).to_broadcast([P, PEER_HEADS, TOPK]),
                    op0=ALU.mult, op1=ALU.mult).then_inc(pick_done, 1)
                dve.wait_ge(pickT_ps, seg + 1)
                nc.vector.tensor_copy(pickT[:, 0:3].rearrange("p r t -> p (r t)"), bank[2][:, 0:3 * P])
                dve.drain()
                nc.vector.tensor_copy(gate_h[:], pickT[:, 2])
                dve.drain()
                nc.vector.tensor_tensor(pickT[:, 3], pickT[:, 2], gate_h[:], ALU.subtract)
                dve.drain().then_inc(pickT_done, 1)

        def g_product(m, i=0):
            s = m % RAW
            dve.wait_ge(act_back[s], 32 * turn(m, i))
            nc.vector.tensor_tensor(g_f[:, m % 2, 0:2 * P], act_in[:, s, 0:2 * P], w_in_t[:, s], ALU.mult)
            nc.vector.tensor_tensor(
                g_f[:, m % 2, 2 * P:].rearrange("p (b t) -> p b t", b=2),
                act_in[:, s, 2 * P:].rearrange("p (b t) -> p b t", b=2),
                w_buf[:, bass.ds(num(m, i), 1)].rearrange("p o b t -> p (o b) t"), ALU.mult).then_inc(g_done, 1)

        def g_low(m, i=0):
            dve.wait_ge(g_hi_done, num(m, i) + 1)
            low_of(g_lo[:, m % 2], g_f[:, m % 2], g_hi[:, m % 2]).then_inc(g_lo_done, 1)

        def v_body(m, i=0):
            g_product(m + 1, i)
            if m + AHEAD < N_EXP:
                lo(FIRST_V + m + AHEAD, i)
            g_low(m + 1, i)

        for m in range(LAST_U, N_EXP):
            if m == N_EXP - 2:
                dve.wait_ge(wbank_free, RING + T // GROUP)
                g_product(0)
            lo(FIRST_U + m + AHEAD)
        g_low(0)
        with dve.Fori(0, V_LOOPS) as i:
            for k in range(STEP):
                v_body(k, i)
        for m in range(V_LOOPS * STEP, N_EXP - 1):
            v_body(m)
        dve.wait_ge(res_back, 16)
        for tt in range(TT + 1):
            if tt < TT:
                ln_moments(res2, tt, TT + tt, UNSCALE)
            if tt >= 1:
                ln_normal(res2, tt - 1, TT + tt - 1)

    @block.gpsimd
    def _(pool):
        nc.gpsimd.memset(cmp_in[:, :, GROUPS, :], 0.0)
        pool.drain().then_inc(zeroed, 1)
        nc.gpsimd.memset(zp[:, :, 0:PAD], 0.0)
        nc.gpsimd.memset(win[:, :, 0:PAD], 0.0)
        pool.drain()

        def copy_cur(g, j):
            rows = slice(g * DH, (g + 1) * DH)
            nc.gpsimd.tensor_copy(q_cur[rows, :], qT[rows, bass.ds(j, 1), :].rearrange("p o t -> p (o t)")
                                  if not isinstance(j, int) else qT[rows, j, :])
            pool.drain().then_inc(q_ready, 1)

        def copy_bias(g, j):
            nc.gpsimd.tensor_copy(bias_cur[:, g, :], bias_all[:, g, bass.ds(j, 1), :].rearrange("p o t -> p (o t)")
                                  if not isinstance(j, int) else bias_all[:, g, j, :])
            pool.drain().then_inc(bias_ready, 1)

        pool.wait_ge(bias_in, 16)
        for g in range(GROUPS):
            copy_bias(g, 0)
        pool.wait_ge(evac, PROJ.index("q3") + 1)
        for g in range(GROUPS):
            copy_cur(g, 0)

        pool.wait_ge(consts_in, 16 * 8)
        pool.wait_ge(evac, N_PROJ)
        pool.drain()
        for g, window in enumerate(POOL_WINDOWS):
            src, shift, w = zp[:, g], 1, 0
            while shift < window:
                nc.gpsimd.tensor_tensor(win[:, w, PAD:], src[:, PAD:], src[:, PAD - shift:PAD + T - shift], ALU.add)
                pool.drain()
                src, w, shift = win[:, w], 1 - w, 2 * shift
            nc.gpsimd.tensor_tensor(win[:, w, PAD:], src[:, PAD:], inv_t[:, g], ALU.mult)
            pool.drain()
            nc.gpsimd.tensor_tensor(zp[:, g, PAD:], win[:, w, PAD:], zp[:, g, PAD:], ALU.subtract).then_inc(y_done, 1)
            pool.drain()

        with pool.Fori(0, PAIRS - 1) as j:
            for g in range(GROUPS):
                pool.wait_ge(s_done, UNITS * j + TT * (g + 1))
                copy_cur(g, j + 1)
                pool.wait_ge(x_done, UNITS * j + TT * (g + 1))
                copy_bias(g, j + 1)

        pool.wait_ge(res_in, 16 * 3)
        for tt in range(TT):
            nc.gpsimd.tensor_scalar(res[:, tt], res[:, tt], ALPHA, 1.0, ALU.mult, ALU.mult)
            pool.drain()
        pool.sem_inc(res_ready, 1)

        def ln_affine(r, g, b, tt, n):
            pool.wait_ge(ln_norm, n + 1)
            nc.gpsimd.tensor_tensor(r[:, tt], r[:, tt], g[:], ALU.mult)
            pool.drain()
            nc.gpsimd.tensor_tensor(r[:, tt], r[:, tt], b[:], ALU.add)
            pool.drain().then_inc(ln_out, 1)

        for tt in range(TT):
            ln_affine(res, lng, lnb, tt, tt)
        def gate_low(tt, st, q):
            pool.wait_ge(eq_done, tt * (P // GROUP) + STEP_GROUPS * st + q + 1)
            rest = pickT[:, 3, bass.ds(TOK_STEP * st + GROUP * q, GROUP)]
            nc.gpsimd.tensor_tensor(oh1[:, q % RING, 1], eq1[:, q % RING],
                                    rest.unsqueeze(2).to_broadcast([P, GROUP, P]), ALU.mult)
            pool.drain().then_inc(oh_lo_done, 1)

        for tt in range(TT):
            pool.wait_ge(pickT_done, tt + 1)
            with pool.Fori(0, SEG_STEPS) as st:
                for q in range(STEP_GROUPS):
                    gate_low(tt, st, q)

        pool.wait_ge(ln2_in, 32)
        for tt in range(TT):
            ln_affine(res2, lng2, lnb2, tt, TT + tt)

    @block.tensor
    def _(pe):
        mm = nc.tensor.matmul

        def three(ps, w_h, w_l, r_h, r_l, start, stop):
            mm(ps, w_h, r_h, start=start, stop=False)
            mm(ps, w_h, r_l, start=False, stop=False)
            return mm(ps, w_l, r_h, start=False, stop=stop)

        def wT_times_aT(b, i=0, x_waits=False):
            s, ps = b % SPLIT, bank[b % 2][:]
            pe.wait_ge(lo_done, num(b, i) + 1)
            for c in range(KC):
                if x_waits and c % 2 == 0:
                    pe.wait_ge(x_lo_done, c // 2 + 1)
                cols = slice(c * P, (c + 1) * P)
                done = three(ps, w_hi[:, s, cols], w_lo[:, s, cols], a_hi[:, c], a_lo[:, c],
                             c == 0, c == KC - 1)
            done.then_inc(tile_used, 1)

        def a_times_w(b):
            s = b % SPLIT
            pe.wait_ge(lo_done, b + 1)
            for tt in range(TT):
                for c in range(KC):
                    cols, toks = slice(c * P, (c + 1) * P), slice(tt * P, (tt + 1) * P)
                    done = three(bank[b % 2][:, toks], a_hi[:, c, toks], a_lo[:, c, toks],
                                 w_hi[:, s, cols], w_lo[:, s, cols], c == 0, c == KC - 1)
            done.then_inc(tile_used, 1)

        def rows_times_tile(b, i, l_hi, l_lo, start, stop, done_sem=None, order=range(TT)):
            s = b % SPLIT
            pe.wait_ge(lo_done, num(b, i) + 1)
            for tt in order:
                if b == FIRST_V and tt == order[-1]:
                    pe.wait_ge(act_done, N_EXP)
                toks = slice(tt * P, (tt + 1) * P)
                for lhs, rhs in ((l_hi, w_hi), (l_hi, w_lo), (l_lo, w_hi)):
                    for half in range(2):
                        done = mm(banks_of(tt)[half][:], lhs[:, toks], rhs[:, s, half * T:(half + 1) * T],
                                  start=start and rhs is w_hi and lhs is l_hi, stop=stop and lhs is l_lo)
                if done_sem is not None and tt < TT - 1:
                    done.then_inc(done_sem, 1)
            if done_sem is not None:
                done.then_inc(done_sem, 1)
            else:
                done.then_inc(tile_used, 1)

        pe.wait_ge(early_in, 16 * 3)
        for half in range(2):
            done = mm(bank[5 + half][0:HEADS, 0:FREV // 2], rel_t[:],
                      onehot_t[:, half * (FREV // 2):(half + 1) * (FREV // 2)], start=True, stop=True)
        done.then_inc(frev_ps, 1)

        for b in range(N_PROJ):
            if b >= 2:
                pe.wait_ge(evac, b - 1)
            if PROJ[b] in ("vslc", "vwin"):
                a_times_w(b)
            else:
                wT_times_aT(b, x_waits=b == 0)
            if b == 6:
                pe.wait_ge(consts_in, 16 * 8)
                for tt in range(TT):
                    for c in range(KC):
                        done = mm(bank[4][:, tt * 24:(tt + 1) * 24], xT_t[:, c, tt * P:(tt + 1) * P],
                                  w_gates_t[:, c], start=c == 0, stop=c == KC - 1)
                done.then_inc(gates_ps, 1)
                pe.wait_ge(cmp_w_in, 16 * 4)
                pe.wait_ge(pe_in, 16)
                half_block = CMP_BLOCK // 2
                for kv in range(2):
                    for mh in range(2):
                        o = (2 * kv + mh) * 3 * N_CMP
                        for bb in range(half_block):
                            blocks = cmp_in[:, kv, :, bb:bb + 8 * (N_CMP - 1) + 1:CMP_STRIDE // 2]
                            done = mm(bank[2][:, o:o + 3 * N_CMP], w1_t[:, kv, bb, mh * P:(mh + 1) * P],
                                      blocks, start=bb == 0, stop=bb == half_block - 1)
                done.then_inc(hid_ps, 1)
            if b == 9:
                pe.wait_ge(hid_done, 1)
                for mh in range(2):
                    mm(bank[3][:, 0:GROUPS * N_CMP], w2k_t[:, mh], hid[:, 0, mh].rearrange("p g n -> p (g n)"),
                       start=mh == 0, stop=mh == 1)
                for g in range(GROUPS):
                    for mh in range(2):
                        done = mm(bank[3][0:N_CMP, 64 + g * DH:64 + (g + 1) * DH], hid[:, 1, mh, g],
                                  w2v_t[:, mh], start=mh == 0, stop=mh == 1)
                done.then_inc(kv_ps, 1)

        pe.wait_ge(evac, N_PROJ)
        pe.wait_ge(kv_done, 1)

        def scores(u, j):
            g, i, par = u // TT, u % TT, u % 2
            rows, n = slice(g * DH, (g + 1) * DH), (i + 1) * P
            if i == 0:
                pe.wait_ge(q_ready, GROUPS * j + g + 1)
            if u >= 2:
                pe.wait_ge(x_done, UNITS * j + u - 1)
            q = q_cur[rows, i * P:(i + 1) * P]
            mm(bank[par][:, 0:n], q, kT_slc[rows, 0:n], start=True, stop=True)
            if i == 0:
                if g > 0:
                    pe.wait_ge(pt_dve, GROUPS * j + g)
                for c in range(TT):
                    mm(bank[4][:, 32 * c:32 * c + n_cmp(c)], q_cur[rows, c * P:(c + 1) * P],
                       kT_cmp[rows, 0:n_cmp(c)], start=True, stop=True)
            mm(bank[2 + par][:, 0:n], q, kT_win[rows, 0:n], start=True, stop=True).then_inc(s_done, 1)

        def transposes(u, j):
            i, par = u % TT, u % 2
            pe.wait_ge(r_done, UNITS * j + u + 1)
            if u >= 1:
                pe.wait_ge(pt_act, UNITS * j + u)
            if i == 0:
                for c in range(TT):
                    nc.tensor.transpose(bank[4][0:N_CMP, c * P:(c + 1) * P], probs_c[:, c, 0:N_CMP],
                                        ident[:])
            for br, ps in ((SLC, bank[5]), (WIN, bank[6])):
                for c in range(i + 1):
                    cols = slice(c * P, (c + 1) * P)
                    done = nc.tensor.transpose(ps[:, cols], probs[:, par, br, cols], ident[:])
            done.then_inc(t_done, 1)

        def outputs(u, j):
            g, i, par = u // TT, u % TT, u % 2
            cols = slice(g * DH, (g + 1) * DH)
            ps = bank[7][cols, i * P:(i + 1) * P]
            if u == 0:
                pe.wait_ge(oT_free, j + 1)
            pe.wait_ge(pt_act, UNITS * j + u + 1)
            if i == 0:
                pe.wait_ge(pt_dve, GROUPS * j + g + 1)
            mm(ps, v_cmp[:, g, :], probsT_c[:, g, i * P:(i + 1) * P], start=True, stop=False)
            for v, br in ((v_slc, SLC), (v_win, WIN)):
                for c in range(i + 1):
                    done = mm(ps, v[:, c, cols], probsT[:, par, br, c * P:(c + 1) * P], start=False,
                              stop=br == WIN and c == i)
            done.then_inc(pv_done, 1)

        with pe.Fori(0, PAIRS) as j:
            scores(0, j)
            for s in range(UNITS + 2):
                if s + 1 < UNITS:
                    scores(s + 1, j)
                if 1 <= s <= UNITS:
                    transposes(s - 1, j)
                if s >= 2:
                    outputs(s - 2, j)

        for g in range(POOL_GROUPS):
            pe.wait_ge(y_done, g + 1)
            mm(bank[g][:], pool_wt[:, g], zp[:, g, PAD:], start=True, stop=True).then_inc(pool_ps, 1)

        pe.wait_ge(pool_lo, POOL_GROUPS)
        pe.wait_ge(oT_free, PAIRS + 1)
        for n, c in enumerate(WOUT_CHUNKS):
            last = n == KC - 1
            rows_times_tile(FIRST_WOUT + n, 0, c_hi[:, c], c_lo[:, c], n == 0, last, mix_done if last else None)
        pe.drain().then_inc(tile_used, 1)
        for tt in range(TT):
            pe.wait_ge(ln_out, tt + 1)
            for c in range(KC):
                done = nc.tensor.transpose(banks_of(tt)[c // 4][:, (c % 4) * P:(c % 4 + 1) * P],
                                           res[:, tt, c * P:(c + 1) * P], ident[:])
            done.then_inc(hT_ps, 1)

        def similarities(hs, i=0):
            pe.wait_ge(q_done, num(hs, i) + 1)
            if hs >= 2:
                pe.wait_ge(sim_sb, num(hs, i) - 1)
            for tt in range(TT):
                toks = slice(tt * P, (tt + 1) * P)
                done = mm(bank[5 + hs % 2][:, toks], q_s[:, hs % 2, toks], subk_t[:, hs % SIDES],
                          start=True, stop=True)
            done.then_inc(sim_ps, 1)

        def query(hs, i=0):
            if hs >= 2:
                pe.wait_ge(q_done, num(hs, i) - 1)
            wT_times_aT(FIRST_WQ + hs, i)
            if hs >= 1:
                similarities(hs - 1, i)

        pe.wait_ge(hT_lo, TT)
        pe.wait_ge(subk_in, 16)
        for hs in range(Q_STRAIGHT):
            query(hs)
        with pe.Fori(0, Q_LOOPS) as i:
            for k in range(STEP):
                query(Q_STRAIGHT + k, i)
        similarities(PEER_HEADS * SIDES - 1)

        pe.sem_inc(wbank_done, RING)

        def experts(m, i=0, later=False):
            if m >= 2 or later:
                pe.wait_ge(act_done, num(m, i) - 1)
            else:
                pe.wait_ge(q_done, PEER_HEADS * SIDES - 1 + m)
            wT_times_aT(FIRST_U + m, i)

        def retrieval(tt, st, q):
            n = tt * (P // GROUP) + STEP_GROUPS * st + q
            pe.wait_ge(oh_hi_done, n + 1)
            pe.wait_ge(oh_lo_done, n + 1)
            pe.wait_ge(wbank_free, n + 1)
            for t in range(GROUP):
                ps = w_bank[q % RING][:, t * P:(t + 1) * P]
                mm(ps, oh2[:, q % RING, t], oh1[:, q % RING, 0, t], start=True, stop=False)
                done = mm(ps, oh2[:, q % RING, t], oh1[:, q % RING, 1, t], start=False, stop=True)
            done.then_inc(wbank_done, 1)

        def step(seg, st, later=False):
            for k in range(STEP):
                experts(seg * SEG_TILES + k, st, later)
                if seg >= 1:
                    for q in GROUPS_AT[k]:
                        retrieval(seg - 1, st, q)

        for seg in range(N_SEG):
            if seg == 0:
                step(0, 0)
                with pe.Fori(1, SEG_STEPS) as st:
                    step(0, st, True)
            else:
                with pe.Fori(0, SEG_STEPS) as st:
                    step(seg, st)
            if seg < N_SEG - 1:
                experts(seg * SEG_TILES + SEG)
                pe.wait_ge(pick_done, seg + 1)
                for row in range(3):
                    done = nc.tensor.transpose(bank[2][:, row * P:(row + 1) * P],
                                               pick3[:, row].rearrange("p h k -> p (h k)"), ident[:])
                done.then_inc(pickT_ps, 1)
        for m in range(LAST_U, N_EXP):
            experts(m)

        pe.wait_ge(wbank_free, RING + T // GROUP)

        def v_tile(m, i=0, start=False, stop=False):
            pe.wait_ge(g_lo_done, num(m, i) + 1)
            rows_times_tile(FIRST_V + m, i, g_hi[:, m % 2], g_lo[:, m % 2], start, stop,
                            mix_done if stop else None, (1, 2, 3, 0) if start else range(TT))

        v_tile(0, 0, start=True)
        with pe.Fori(0, V_LOOPS) as i:
            for k in range(STEP):
                v_tile(k + 1, i)
        for m in range(V_LOOPS * STEP + 1, N_EXP):
            v_tile(m, 0, stop=m == N_EXP - 1)

    return ctx


def _bucket(dist):
    d = np.maximum(dist, 0)
    exact = N_BUCKETS // 2
    f = np.float32
    big = exact + (np.log(np.maximum(d, 1).astype(f) / f(exact)) / f(np.log(MAX_DISTANCE / exact))
                   * f(N_BUCKETS - exact)).astype(np.int32)
    return np.where(d < exact, d, np.minimum(big, N_BUCKETS - 1))


def kernel(x, w_in, rel_table, cmp_pe_k, cmp_pe_v, cmp_k_w1, cmp_k_w2, cmp_v_w1, cmp_v_w2, pool_w,
           pool_scale, w_out, ln1_g, ln1_b, peer_wq, peer_subkeys, peer_u, peer_v, ln2_g, ln2_b):
    import concourse.bacc as bacc
    from concourse.bass_utils import run_bass_kernel_spmd

    x, w_in, w_out, wq, u, v = (np.asarray(a)[0] for a in (x, w_in, w_out, peer_wq, peer_u, peer_v))
    nsa, kv = HEADS * DH, GROUPS * DH
    names = ["kc", "vc", "kslc", "vslc", "kwin", "vwin"]
    at = {n: nsa + kv * i for i, n in enumerate(names)}
    gate0 = nsa + 6 * kv
    z0 = gate0 + 3 * HEADS
    cols = []
    for name in PROJ:
        if name[:2] in ("kc", "vc"):
            g = int(name[2])
            one = list(range(at[name[:2]] + g * DH, at[name[:2]] + (g + 1) * DH))
            cols += one + one
        elif name[0] == "q":
            j = int(name[1])
            cols += [h * DH + d for h in (j, j + PAIRS) for d in range(DH)]
        elif name[0] == "z":
            cols += list(range(z0 + int(name[1]) * P, z0 + (int(name[1]) + 1) * P))
        else:
            cols += list(range(at[name], at[name] + P))

    def column_tiles(w):
        return w.reshape(KC, P, -1, P).transpose(2, 1, 0, 3).reshape(-1, P, D)

    rows = []
    for c in WOUT_CHUNKS:
        if c < PAIRS:
            rows += [h * DH + d for h in (c, c + PAIRS) for d in range(DH)]
        else:
            rows += list(range(c * P, (c + 1) * P))
    stream = np.empty((N_TILES, P, D), np.float32)
    stream[:FIRST_WOUT] = column_tiles(w_in[:, cols])
    stream[FIRST_WOUT:FIRST_WQ] = w_out[rows].reshape(KC, P, D)
    stream[FIRST_WQ:FIRST_U] = column_tiles(wq)
    stream[FIRST_U:FIRST_V] = u.reshape(N_EXP, P, KC, P).transpose(0, 3, 2, 1).reshape(N_EXP, P, D)
    stream[FIRST_V:] = v.reshape(N_EXP, P, D)

    dist = T - 1 - np.arange(FREV)
    onehot = np.zeros((N_BUCKETS + 1, FREV), np.float32)
    onehot[_bucket(dist), np.arange(FREV)] = 1.0
    onehot[:, dist < 0] = 0.0
    onehot[N_BUCKETS, dist < 0] = 1.0
    counts = np.stack([1.0 / np.minimum(np.arange(T) + 1, w) for w in POOL_WINDOWS]).astype(np.float32)

    def every_row(a):
        return np.ascontiguousarray(np.broadcast_to(a, (P,) + a.shape))

    def pe_rows(a):
        return np.asarray(a)[0].reshape(CMP_BLOCK // 2, P).T

    w2k = np.asarray(cmp_k_w2)[0].reshape(2, P, DH).transpose(1, 0, 2)
    arrays = {
        "x": x[0] if x.ndim == 3 else x,
        "xT": (x[0] if x.ndim == 3 else x).T.reshape(KC, P, T).transpose(1, 0, 2),
        "stream": stream,
        "w_gates": w_in[:, gate0:z0].reshape(KC, P, 3 * HEADS).transpose(1, 0, 2),
        "rel": np.asarray(rel_table),
        "rel_neg": np.full((1, HEADS), NEG, np.float32),
        "onehot": onehot,
        "w1": np.stack([np.asarray(a)[0].reshape(CMP_BLOCK // 2, P, CMP_HIDDEN).transpose(1, 0, 2)
                        for a in (cmp_k_w1, cmp_v_w1)]),
        "w2k": np.concatenate([w2k, w2k], axis=2),
        "w2v": np.asarray(cmp_v_w2)[0].reshape(2, P, DH).transpose(1, 0, 2),
        "pe_kv": np.stack([pe_rows(cmp_pe_k), pe_rows(cmp_pe_v)], axis=1),
        "pool_w": np.asarray(pool_w)[0].transpose(1, 0, 2),
        "pool_scale": np.asarray(pool_scale)[0].reshape(POOL_GROUPS, P).T,
        "inv_cnt": every_row(counts),
        "row_ok": (np.arange(P) >= CMP_BLOCK - 1).astype(np.float32).reshape(P, 1),
        "ln1_g": every_row(np.asarray(ln1_g)[0]),
        "ln1_b": every_row(np.asarray(ln1_b)[0]),
        "subkeys": np.asarray(peer_subkeys)[0].transpose(2, 0, 1),
        "ln2_g": every_row(np.asarray(ln2_g)[0]),
        "ln2_b": every_row(np.asarray(ln2_b)[0]),
        "eye": np.eye(P, dtype=np.float32),
        "iota_h": every_row(np.arange(P).astype(np.float16)),
        "iota16": every_row(np.arange(TOPK).astype(np.float32)),
    }
    nc = bacc.Bacc("TRN2", target_bir_lowering=False, num_devices=1)
    inputs, args = {}, []
    for name, a in arrays.items():
        a = np.ascontiguousarray(a)
        inputs[f"in_{name}"] = a
        args.append(nc.dram_tensor(f"in_{name}", a.shape, mybir.dt.from_np(a.dtype), kind="ExternalInput").ap())
    args.append(nc.dram_tensor("out", (T, D), F32, kind="ExternalOutput").ap())
    for name, shape in (("bias_rows", (HEADS, P, FREV)), ("gelu_act", (N_EXP, P, T)),
                        ("retrieval", (P, N_EXP, 2 * P)), ("residual", (T, D))):
        args.append(nc.dram_tensor(name, shape, F32, kind="Internal").ap())
    layer(nc, *args).close()
    r = run_bass_kernel_spmd(nc, [inputs], core_ids=[0])
    return r.results[0]["out"].reshape(1, T, D)
```

```python
from contextlib import ExitStack

import numpy as np
import concourse.bass as bass
from concourse import mybir

P = 128
T = 512
D = 1024
TT = T // P
KC = D // P
HEADS, GROUPS, DH = 8, 2, 64
PAIRS = HEADS // GROUPS
UNITS = GROUPS * TT
CMP_BLOCK, CMP_STRIDE, CMP_HIDDEN = 32, 16, 256
N_CMP = (T - CMP_BLOCK) // CMP_STRIDE + 1
ROWS_OF_G = T // CMP_STRIDE
N_ROWS = GROUPS * ROWS_OF_G + 1
N_BUCKETS, MAX_DISTANCE = 32, 128
NEG = -1e30
POOL_WINDOWS = (2, 4, 8, 16)
POOL_GROUPS = len(POOL_WINDOWS)
PAD = max(POOL_WINDOWS)
PEER_HEADS, SIDES, TOPK = 8, 2, 16
N_EXP = 128
ALPHA = 2 ** 0.25
LN_EPS = 1e-5
LOWEST, HIGHEST = -3.0e38, 3.0e38

ACT_SCALE = 16.0
W_SCALE = 128.0
GATE_SCALE = 256.0
UNSCALE = 1.0 / (ACT_SCALE * W_SCALE)

FREV = 640
RAW = 3
SPLIT = 3
STEP = 6

F32, F16, U32 = mybir.dt.float32, mybir.dt.float16, mybir.dt.uint32
ALU, ACTF = mybir.AluOpType, mybir.ActivationFunctionType
AX_X = mybir.AxisListType.X

PROJ = ["kc0", "kc1", "vc0", "vc1", "vslc", "vwin", "kslc", "kwin",
        "q0", "q1", "q2", "q3", "z0", "z1", "z2", "z3"]
N_PROJ = len(PROJ)
WOUT_CHUNKS = [4, 5, 6, 7, 0, 1, 2, 3]
FIRST_WOUT = N_PROJ
FIRST_WQ = FIRST_WOUT + KC
FIRST_U = FIRST_WQ + PEER_HEADS * SIDES
FIRST_V = FIRST_U + N_EXP
N_TILES = FIRST_V + N_EXP
Q_STRAIGHT = (PEER_HEADS * SIDES) % STEP
Q_LOOPS = (PEER_HEADS * SIDES) // STEP
V_LOOPS = (N_EXP - RAW) // STEP
AHEAD = SPLIT - 1

SEG_STEPS = 4
SEG = SEG_STEPS * STEP
SEG_TILES = SEG + 1
N_SEG = TT + 1
LAST_U = SEG * N_SEG + TT
TOK_STEP = P // SEG_STEPS
GROUP = 4
STEP_GROUPS = TOK_STEP // GROUP
RING = 4
ROWS_AT = [[0, 1], [2], [3, 4], [5], [6, 7], []]
GROUPS_AT = [[0], [1], [2], [3, 4], [5], [6, 7]]
assert N_EXP - LAST_U > AHEAD

SLC, WIN = range(2)
QK = ["kslc", "kwin", "q0", "q1", "q2", "q3"]
QK_SCALE = {"q": UNSCALE * DH ** -0.5, "k": UNSCALE}
POOL_BANKS = [0, 2, 1, 3]
GATE_CMP = 0


def n_cmp(i):
    return (i + 1) * P // CMP_STRIDE - 1


def layer(nc, x, xT, stream, w_gates, rel, rel_neg, onehot, w1, w2k, w2v, pe_kv, pool_w, pool_scale,
          inv_cnt, row_ok, ln1_g, ln1_b, ln1_gb, subkeys, ln2_g, ln2_b, eye, spread, iota_h, iota16, out,
          frev_d, act_d, w_d, res_d):
    ctx, front, first, attn, peer, stage_a, stage_b = (ExitStack() for _ in range(7))

    def sb(name, shape, dt=F32, scope=ctx):
        return scope.enter_context(nc.sbuf_tensor(name, shape, dt))

    def sem(name):
        return ctx.enter_context(nc.semaphore(name))

    raw = sb("raw", [P, RAW, D])
    w_hi = sb("w_hi", [P, SPLIT, D], F16)
    w_lo = sb("w_lo", [P, SPLIT, D], F16)
    a_hi = sb("a_hi", [P, KC, T], F16)
    a_lo = sb("a_lo", [P, KC, T], F16)
    ident = sb("ident", [P, P])
    iota_t = sb("iota_t", [P, P], F16)
    iota16_t = sb("iota16_t", [P, TOPK])
    ln_stats = sb("ln_stats", [P, 2, 6])
    ln_mv = sb("ln_mv", [P, TT, 2])
    ln_rstd = sb("ln_rstd", [P, TT, 3])
    eps_t = sb("eps_t", [P, 1])

    xT_t = sb("xT_t", [P, KC, T], F32, first)
    w1_t = sb("w1_t", [P, 2, CMP_BLOCK // 2, CMP_HIDDEN], F32, first)
    rel_t = sb("rel_t", [N_BUCKETS + 1, HEADS], F32, first)
    onehot_t = sb("onehot_t", [N_BUCKETS + 1, FREV], F32, first)
    frev = sb("frev", [HEADS, FREV], F32, first)
    cmp_in = sb("cmp_in", [P, 2, GROUPS * (T // 2) + CMP_BLOCK // 2], F32, first)
    hid = sb("hid", [P, 2, 2, GROUPS, N_CMP], F32, first)
    hid_pre = sb("hid_pre", [P, 2, CMP_HIDDEN], F32, first)
    wg_hi, wg_lo = (hid_pre[:, i].bitcast(F16)[:, 0:KC * 3 * HEADS].rearrange("p (c n) -> p c n", c=KC)
                    for i in range(2))
    spread_t = sb("spread_t", [N_ROWS, GROUPS * N_CMP], F32, first)
    w2k_t = sb("w2k_t", [P, 2, P], F32, first)
    w2v_t = sb("w2v_t", [P, 2, DH], F32, first)
    w_gates_t = sb("w_gates_t", [P, KC, 3 * HEADS], F32, first)
    first_end = nc.sbuf_base
    first.close()
    neg_x = sb("neg_x", [P, 2, 2, T], F32, attn)
    hT_f = neg_x[:].rearrange("p s b k -> p s (b k)").rearrange("p s (c t) -> p s c t", c=KC)
    probs = sb("probs", [P, 2, 2, T], F32, attn)
    probsT = sb("probsT", [P, 2, 2, T], F32, attn)
    neg_max = sb("neg_max", [P, 2, 2], F32, attn)
    row_sum = sb("row_sum", [P, 2, 2], F32, attn)
    row_scale = sb("row_scale", [P, 2, 2, 2], F32, attn)
    neg_xc = sb("neg_xc", [P, TT, 32], F32, attn)
    probs_c = sb("probs_c", [P, TT, 32], F32, attn)
    probsT_c = sb("probsT_c", [N_CMP, GROUPS, T], F32, attn)
    neg_max_c = sb("neg_max_c", [P, TT], F32, attn)
    row_sum_c = sb("row_sum_c", [P, TT], F32, attn)
    row_scale_c = sb("row_scale_c", [P, 2, TT], F32, attn)
    attn_end = nc.sbuf_base
    attn.close()
    sb("front_gap", [P, (max(first_end, attn_end) - nc.sbuf_base + 3) // 4], F32, front)
    bias_all = sb("bias_all", [P, GROUPS, PAIRS, T], F32, front)
    bias_cur = sb("bias_cur", [P, GROUPS, T], F32, front)
    q_two = sb("q_two", [P, PAIRS, GROUPS, T], F16, front)
    k_two = sb("k_two", [P, 2, GROUPS, T], F16, front)
    k_low = sb("k_low", [P, 2, GROUPS, T], F16, front)
    v_slc = sb("v_slc", [P, TT, P], F32, front)
    v_win = sb("v_win", [P, TT, P], F32, front)
    gates = sb("gates", [P, TT, 3, HEADS], F32, front)
    kc_two = sb("kc_two", [P, GROUPS, N_CMP], F16, front)
    kc_low = sb("kc_low", [P, GROUPS, N_CMP], F16, front)
    v_cmp = sb("v_cmp", [N_CMP, GROUPS, DH], F32, front)
    zp = sb("zp", [P, POOL_GROUPS, PAD + T], F32, front)
    win = sb("win", [P, 2, PAD + T], F32, front)
    inv_t = sb("inv_t", [P, POOL_GROUPS, T], F32, front)
    pool_wt = sb("pool_wt", [P, POOL_GROUPS, P], F32, front)
    pool_sc = sb("pool_sc", [P, POOL_GROUPS], F32, front)
    pool_sc16 = sb("pool_sc16", [P, POOL_GROUPS], F32, front)
    row_ok_t = sb("row_ok_t", [P, 1], F32, front)
    c_hi = sb("c_hi", [P, KC, T], F16, front)
    c_lo = sb("c_lo", [P, KC, T], F16, front)
    q_moves = c_lo[:, 0:PAIRS]
    lng = sb("lng", [P, D], F32, front)
    lnb = sb("lnb", [P, D], F32, front)
    ln_gb = sb("ln_gb", [P, 2, KC], F32, front)
    ln_gb16 = sb("ln_gb16", [P, 2, KC], F32, front)
    res = sb("res", [P, TT, D], F32, front)
    front.close()

    w_buf = sb("w_buf", [P, N_EXP, 2, P], F32, peer)
    picks_v = sb("picks_v", [P, TT, PEER_HEADS, SIDES, TOPK], F32, stage_a)
    picks_i = sb("picks_i", [P, TT, PEER_HEADS, SIDES, TOPK], F32, stage_a)
    best_v = sb("best_v", [P, TOPK], F32, stage_a)
    best_i = sb("best_i", [P, TOPK], U32, stage_a)
    best_ab = sb("best_ab", [P, SIDES, TOPK], U32, stage_a)
    eq = sb("eq", [P, SIDES, TOPK, TOPK], F32, stage_a)
    cand, cand_r = eq[:, 0], eq[:, 1]
    score = sb("score", [P, PEER_HEADS, TOPK], F32, stage_a)
    gsum = sb("gsum", [P, 2, PEER_HEADS], F32, stage_a)
    pick3 = sb("pick3", [P, 3, PEER_HEADS, TOPK], F32, stage_a)
    pickT = sb("pickT", [P, 4, P], F32, stage_a)
    gate_h = sb("gate_h", [P, P], F16, stage_a)
    pick_cur = sb("pick_cur", [P, 2, TOK_STEP], F32, stage_a)
    gate_cur = sb("gate_cur", [P, TOK_STEP], F32, stage_a)
    oh2 = sb("oh2", [P, RING, GROUP, P], F16, stage_a)
    eq1 = sb("eq1", [P, RING, GROUP, P], F16, stage_a)
    oh1 = sb("oh1", [P, RING, 2, GROUP, P], F16, stage_a)
    act_out = sb("act_out", [P, RAW, T], F32, stage_a)
    stage_a.close()
    act_in = sb("act_in", [P, RAW, T], F32, stage_b)
    w_in_t = sb("w_in_t", [P, RAW, 2 * P], F32, stage_b)
    g_f = sb("g_f", [P, SPLIT, T], F32, stage_b)
    g_hi = sb("g_hi", [P, SPLIT, T], F16, stage_b)
    g_lo = sb("g_lo", [P, SPLIT, T], F16, stage_b)
    lng2 = sb("lng2", [P, D], F32, stage_b)
    lnb2 = sb("lnb2", [P, D], F32, stage_b)
    stage_b.close()
    peer.close()
    wv = w_buf[:].rearrange("p a b c -> p (a b c)")
    q_s = wv[:, 0:2 * T].rearrange("p (s t) -> p s t", s=2)
    sim = wv[:, 2 * T:4 * T].rearrange("p (s t k) -> p s t k", s=2, t=TT)
    sim_r = wv[:, 4 * T:5 * T].rearrange("p (t k) -> p t k", t=TT)
    subk_t = wv[:, 5 * T:5 * T + 2 * P].rearrange("p (s k) -> p s k", s=2)
    top_v = wv[:, 6 * T:6 * T + TT * TOPK].rearrange("p (t k) -> p t k", t=TT)
    top_i = wv[:, 6 * T + P:6 * T + P + TT * TOPK].bitcast(U32).rearrange("p (t k) -> p t k", t=TT)
    res2 = wv[:, 0:TT * D].rearrange("p (t d) -> p t d", t=TT)

    bank = [ctx.enter_context(nc.psum_tensor(f"bank{i}", [P, 512], F32)) for i in range(8)]
    w_bank = bank[8 - RING:]

    raw_in = [sem(f"raw_in{s}") for s in range(RAW)]
    hi_done, lo_done, tile_used = sem("hi_done"), sem("lo_done"), sem("tile_used")
    x_in = [sem(f"x_in{c}") for c in range(4)]
    x_hi_done, x_lo_done = sem("x_hi_done"), sem("x_lo_done")
    early_in, frev_ps, frev_sb, frev_out, bias_in = (
        sem(s) for s in ("early_in", "frev_ps", "frev_sb", "frev_out", "bias_in"))
    inv_in = sem("inv_in")
    cmp_w_in, pe_in, consts_in, res_in = sem("cmp_w_in"), sem("pe_in"), sem("consts_in"), sem("res_in")
    evac = sem("evac")
    wg_hi_done, wg_done = sem("wg_hi_done"), sem("wg_done")
    gates_ps, gates_exp = sem("gates_ps"), sem("gates_exp")
    hid_ps, hid_pre_done, hid_T, hid_done = (sem(s) for s in ("hid_ps", "hid_pre_done", "hid_T", "hid_done"))
    kv_ps, kv_done, kc_done = sem("kv_ps"), sem("kv_done"), sem("kc_done")
    low_evac = sem("low_evac")
    res_ready, y_done, pool_ps, pool_hi, pool_lo = (
        sem(s) for s in ("res_ready", "y_done", "pool_ps", "pool_hi", "pool_lo"))
    dup_done = sem("dup_done")
    bias_ready = sem("bias_ready")
    s_done = sem("s_done")
    x_done = sem("x_done")
    e_done = sem("e_done")
    r_done = sem("r_done")
    t_done = sem("t_done")
    pt_act, pt_cmp = sem("pt_act"), sem("pt_cmp")
    pv_done = sem("pv_done")
    oT_hi, oT_free = sem("oT_hi"), sem("oT_free")
    mix_done = sem("mix_done")
    ln_var, ln_std, ln_scale, ln_norm = (sem(s) for s in ("ln_var", "ln_std", "ln_scale", "ln_norm"))
    ln_gain, ln_out = sem("ln_gain"), sem("ln_out")
    hT_ps, hT_affine, hT_lo = sem("hT_ps"), sem("hT_affine"), sem("hT_lo")
    res_alpha, res_out, subk_in = sem("res_alpha"), sem("res_out"), sem("subk_in")
    q_done, sim_ps, sim_sb, top_done = sem("q_done"), sem("sim_ps"), sem("sim_sb"), sem("top_done")
    score_done, exp_done, pick_done, pickT_ps, pickT_free = (
        sem(s) for s in ("score_done", "exp_done", "pick_done", "pickT_ps", "pickT_free"))
    eq_done, oh_hi_done, oh_lo_done, pickT_done, wbank_done, wbank_free = (
        sem(s) for s in ("eq_done", "oh_hi_done", "oh_lo_done", "pickT_done", "wbank_done", "wbank_free"))
    w_saved = [sem(f"w_saved{s}") for s in range(2)]
    act_done = sem("act_done")
    act_saved = [sem(f"act_saved{s}") for s in range(RAW)]
    act_back = [sem(f"act_back{s}") for s in range(RAW)]
    g_done, g_hi_done, g_lo_done = sem("g_done"), sem("g_hi_done"), sem("g_lo_done")
    last_half = sem("last_half")
    ln2_in, res_back, out_saved = sem("ln2_in"), sem("res_back"), sem("out_saved")

    block = ctx.enter_context(nc.Block())

    def first_units(u, j):
        return u < 2 and isinstance(j, int) and j == 0

    def branch(u, j, br):
        return 2 * (UNITS * j + u) + br + 1

    def num(b, i):
        return b + STEP * i

    def turn(b, i):
        return b // RAW + (STEP // RAW) * i + 1

    def banks_of(tt):
        return bank[2 * tt], bank[2 * tt + 1]

    def group_rows(g):
        return slice(g * DH, (g + 1) * DH)

    def q_high(j, g):
        return q_two[0:DH, j, 0] if g == 0 else q_moves[DH:P, j]

    def hid_bank(kv, mh):
        o = (2 * kv + mh) * GROUPS * N_CMP
        return bank[3][:, o:o + GROUPS * N_CMP]

    def hT_banks(tt):
        return banks_of((1, 2, 3, 1)[tt])

    @block.sync
    def _(sp):
        def load_tile(b, i=0):
            sp.dma_start(raw[:, b % RAW], stream[num(b, i)]).then_inc(raw_in[b % RAW], 16)

        def next_tile(b, i=0):
            sp.wait_ge(lo_done, num(b, i) + 1)
            load_tile(b + RAW, i)

        for c in range(4):
            sp.dma_start(xT_t[:, 2 * c:2 * c + 2], xT[:, 2 * c:2 * c + 2]).then_inc(x_in[c], 16)
            if c < RAW:
                load_tile(c)
            if c == 1:
                sp.dma_start(rel_t[0:N_BUCKETS, :], rel).then_inc(early_in, 16)
                sp.dma_start(rel_t[N_BUCKETS:N_BUCKETS + 1, :], rel_neg).then_inc(early_in, 16)
                sp.dma_start(onehot_t[:], onehot).then_inc(early_in, 16)
        for b in range(N_PROJ):
            next_tile(b)
            if b == 0:
                sp.dma_start(cmp_in[:, :, GROUPS * (T // 2):], pe_kv).then_inc(pe_in, 16)
                for dst, src in ((w_gates_t, w_gates), (w2k_t, w2k), (w2v_t, w2v), (spread_t, spread)):
                    sp.dma_start(dst[:], src).then_inc(cmp_w_in, 16)
            if b in (1, 2):
                sp.dma_start(w1_t[:, b - 1], w1[b - 1]).then_inc(cmp_w_in, 16)
            if b == 3:
                for dst, src in ((ident, eye), (row_ok_t, row_ok), (pool_wt, pool_w), (pool_sc, pool_scale),
                                 (iota_t, iota_h), (iota16_t, iota16)):
                    sp.dma_start(dst[:], src).then_inc(consts_in, 16)
            if b == 5:
                sp.wait_ge(frev_sb, 1)
                sp.dma_start(frev_d, frev[:].unsqueeze(1).to_broadcast([HEADS, P, FREV])).then_inc(frev_out, 16)
            if b == 8:
                sp.wait_ge(frev_out, 16)
                skew = bass.AP(frev_d.tensor, P - 1, [[FREV - 1, P], [P * FREV, HEADS], [1, T]])
                sp.dma_start(bias_all[:].rearrange("p g j t -> p (g j) t"), skew).then_inc(bias_in, 16)
            if b >= 3 and PROJ[b - 3] in QK:
                name = PROJ[b - 3]
                i = QK.index(name)
                sp.wait_ge(low_evac, i + 1)
                upper, lower = group_rows(0), group_rows(1)
                if name[0] == "q":
                    moves = ((q_two[lower, i - 2, 0], q_moves[upper, i - 2]),
                             (q_two[upper, i - 2, 1], q_moves[lower, i - 2]))
                else:
                    moves = ((k_two[lower, i, 0], k_two[upper, i, 0]),
                             (k_two[upper, i, 1], k_two[lower, i, 1]),
                             (k_low[upper, i, 1], k_low[lower, i, 1]))
                for dst, src in moves:
                    sp.dma_start(dst, src).then_inc(dup_done, 16)
            if b == 10:
                sp.dma_start(inv_t[:], inv_cnt).then_inc(inv_in, 16)
        sp.dma_start(res[:], x.rearrange("(t p) d -> p t d", p=P)).then_inc(res_in, 16)
        sp.dma_start(lng[:], ln1_g).then_inc(res_in, 16)
        sp.dma_start(lnb[:], ln1_b).then_inc(res_in, 16)
        sp.dma_start(ln_gb[:], ln1_gb).then_inc(res_in, 16)
        for b in range(FIRST_WOUT, FIRST_WQ):
            next_tile(b)
            if b == FIRST_WOUT:
                sp.wait_ge(oT_free, PAIRS + 1)
                sp.dma_start(subk_t, subkeys).then_inc(subk_in, 16)
        for b in range(FIRST_WQ, FIRST_WQ + Q_STRAIGHT):
            next_tile(b)
            if b == FIRST_WQ + 1:
                sp.wait_ge(res_alpha, TT)
                sp.dma_start(res_d.rearrange("(t p) d -> p t d", p=P), res[:]).then_inc(res_out, 16)
        with sp.Fori(0, Q_LOOPS) as i:
            for k in range(STEP):
                next_tile(FIRST_WQ + Q_STRAIGHT + k, i)

        def save_act(m, i=0):
            sp.wait_ge(act_done, num(m, i) + 1)
            sp.dma_start(act_d[num(m, i)], act_out[:, m % RAW]).then_inc(act_saved[m % RAW], 16)

        def save_w(tt, st, quarter):
            i1 = (N_EXP // SEG_STEPS) * st + 8 * quarter
            sp.dma_start(w_d[:, bass.ds(i1, 8), tt * P:(tt + 1) * P],
                         w_buf[:, bass.ds(i1, 8), tt % 2, :]).then_inc(w_saved[tt], 16)

        def step(seg, st, m0=0):
            base = seg * SEG_TILES
            for k in range(STEP):
                next_tile(FIRST_U + base + k, st)
                if base + k > 0:
                    save_act(base + k - 1, st)
                elif m0:
                    save_act(base + k - 1, st)
                if seg in (2, 3) and k in (1, 2, 4, 5):
                    save_w(seg - 2, st, (1, 2, 4, 5).index(k))

        def load_g(m, i=0):
            s = m % RAW
            sp.dma_start(act_in[:, s], act_d[num(m, i)]).then_inc(act_back[s], 16)
            sp.dma_start(w_in_t[:, s], w_d[:, num(m, i)]).then_inc(act_back[s], 16)

        for seg in range(N_SEG):
            if seg == 0:
                step(0, 0)
                with sp.Fori(1, SEG_STEPS) as st:
                    step(0, st, 1)
            else:
                if seg in (2, 3):
                    sp.wait_ge(wbank_free, RING + (seg - 1) * (P // GROUP))
                with sp.Fori(0, SEG_STEPS) as st:
                    step(seg, st)
            if seg < N_SEG - 1:
                m = seg * SEG_TILES + SEG
                next_tile(FIRST_U + m)
                save_act(m - 1)
            if seg == TT - 1:
                for s in range(2):
                    sp.wait_ge(w_saved[s], 16 * 16)
                for s in range(RAW):
                    sp.wait_ge(act_saved[s], 16 * ((m - s + RAW - 1) // RAW))
                sp.wait_ge(pickT_done, TT)
                for g in range(RAW):
                    load_g(g)
        for m in range(LAST_U, N_EXP):
            next_tile(FIRST_U + m)
            save_act(m - 1)
            if m == LAST_U:
                sp.wait_ge(wbank_free, RING + T // GROUP)
                sp.dma_start(lng2[:], ln2_g).then_inc(ln2_in, 16)
                sp.dma_start(lnb2[:], ln2_b).then_inc(ln2_in, 16)
        save_act(N_EXP - 1)
        for s in range(RAW):
            sp.wait_ge(act_saved[s], 16 * ((N_EXP - s + RAW - 1) // RAW))

        def v_body(m, i=0):
            next_tile(FIRST_V + m, i)
            sp.wait_ge(g_done, num(m, i) + 1)
            load_g(m + RAW, i)

        with sp.Fori(0, V_LOOPS) as i:
            for k in range(STEP):
                v_body(k, i)
        sp.dma_start(res2, res_d.rearrange("(t p) d -> p t d", p=P)).then_inc(res_back, 16)
        for m in range(V_LOOPS * STEP, N_EXP - RAW):
            v_body(m)
        for tt in range(TT - 1):
            sp.wait_ge(ln_out, tt + 1)
            sp.dma_start(out[tt * P:(tt + 1) * P, :], res2[:, tt]).then_inc(out_saved, 16)
        for half in range(2):
            sp.wait_ge(last_half, half + 1)
            sp.dma_start(out[(TT - 1) * P:, half * T:(half + 1) * T],
                         res2[:, TT - 1, half * T:(half + 1) * T]).then_inc(out_saved, 16)
        sp.wait_ge(out_saved, 16 * (TT + 1))

    @block.scalar
    def _(act):
        def hi(b, i=0):
            act.wait_ge(raw_in[b % RAW], 16 * turn(b, i))
            if b >= SPLIT:
                act.wait_ge(tile_used, num(b, i) - SPLIT + 1)
            nc.scalar.activation(w_hi[:, b % SPLIT], raw[:, b % RAW], ACTF.Copy,
                                 scale=W_SCALE).then_inc(hi_done, 1)

        for c in range(4):
            act.wait_ge(x_in[c], 16)
            nc.scalar.activation(a_hi[:, 2 * c:2 * c + 2], xT_t[:, 2 * c:2 * c + 2], ACTF.Copy,
                                 scale=ACT_SCALE).then_inc(x_hi_done, 1)
            if c < AHEAD:
                hi(c)

        def copy_out(b):
            name, ps = PROJ[b], bank[b % 2]
            act.wait_ge(tile_used, b + 1)
            if name[:2] in ("kc", "vc"):
                kv, g = int(name[0] == "v"), int(name[2])
                two, toks = ps[:].rearrange("p (t o) -> p t o", o=2), slice(g * (T // 2), (g + 1) * (T // 2))
                nc.scalar.activation(cmp_in[0:DH, kv, toks], two[0:DH, :, 0], ACTF.Copy, scale=UNSCALE)
                done = nc.scalar.activation(cmp_in[DH:P, kv, toks], two[DH:P, :, 1], ACTF.Copy,
                                            scale=UNSCALE)
            elif name[0] == "z":
                done = nc.scalar.activation(zp[:, int(name[1]), PAD:], ps[:], ACTF.Copy, scale=UNSCALE)
            elif name[0] == "q":
                for g in range(GROUPS):
                    done = nc.scalar.activation(q_high(int(name[1]), g), ps[group_rows(g)],
                                                ACTF.Copy, scale=QK_SCALE["q"])
            elif name in QK:
                for g in range(GROUPS):
                    done = nc.scalar.activation(k_two[group_rows(g), QK.index(name), g], ps[group_rows(g)],
                                                ACTF.Copy, scale=QK_SCALE["k"])
            else:
                dst = {"vslc": v_slc[:].rearrange("p t d -> p (t d)"),
                       "vwin": v_win[:].rearrange("p t d -> p (t d)")}[name]
                done = nc.scalar.activation(dst, ps[:], ACTF.Copy, scale=UNSCALE)
            done.then_inc(evac, 1)

        for b in range(N_PROJ):
            hi(b + AHEAD)
            copy_out(b)
            if b == 4:
                act.wait_ge(cmp_w_in, 16 * 6)
                nc.scalar.activation(wg_hi, w_gates_t[:], ACTF.Copy, scale=W_SCALE).then_inc(wg_hi_done, 1)
            if b == 8:
                act.wait_ge(gates_ps, 1)
                nc.scalar.activation(gates[:].rearrange("p t b h -> p t (b h)"),
                                     bank[4][:, 0:TT * 3 * HEADS].rearrange("p (t n) -> p t n", t=TT),
                                     ACTF.Exp, scale=-UNSCALE).then_inc(gates_exp, 1)
                act.wait_ge(hid_T, 1)
                for kv in range(2):
                    for mh in range(2):
                        done = nc.scalar.activation(hid[:, kv, mh].rearrange("p g n -> p (g n)"),
                                                    hid_bank(kv, mh), ACTF.Gelu)
                done.then_inc(hid_done, 1)
            if b == 10:
                act.wait_ge(kv_ps, 1)
                nc.scalar.copy(kc_two[:].rearrange("p g n -> p (g n)"), bank[2][:, 0:GROUPS * N_CMP])
                nc.scalar.copy(v_cmp[:].rearrange("n g d -> n (g d)"),
                               bank[2][0:N_CMP, 64:64 + GROUPS * DH]).then_inc(kv_done, 1)

        def exps(u, j):
            i, par = u % TT, u % 2
            if not first_units(u, j):
                act.wait_ge(t_done, branch(u - 2, j, WIN))
            n = (i + 1) * P
            for br in (SLC, WIN):
                act.wait_ge(x_done, branch(u, j, br))
                if i == 0 and br == WIN:
                    nc.scalar.activation(probs_c[:], probs_c[:], ACTF.Exp, scale=-1.0)
                nc.scalar.activation(probs[:, par, br, 0:n], neg_x[:, par, br, 0:n], ACTF.Exp,
                                     scale=-1.0, bias=neg_max[:, par, br:br + 1],
                                     accum_out=row_sum[:, par, br:br + 1]).then_inc(e_done, 1)

        def copy_pT(u, j):
            i, par = u % TT, u % 2
            if not first_units(u, j):
                act.wait_ge(pv_done, UNITS * j + u - 1)
            for br, ps in ((SLC, bank[5]), (WIN, bank[6])):
                act.wait_ge(t_done, branch(u, j, br))
                if i == 0 and br == SLC:
                    nc.scalar.copy(probsT_c[:, u // TT, :], bank[4][0:N_CMP, :]).then_inc(pt_cmp, 1)
                nc.scalar.copy(probsT[:, par, br, 0:(i + 1) * P], ps[:, 0:(i + 1) * P]).then_inc(pt_act, 1)

        def oT_high(j):
            act.wait_ge(pv_done, UNITS * j + UNITS)
            nc.scalar.activation(c_hi[:, j, :], bank[7][:], ACTF.Copy, scale=ACT_SCALE).then_inc(oT_hi, 1)

        for u in range(3):
            exps(u, 0)
            if u >= 1:
                copy_pT(u - 1, 0)
        with act.Fori(0, PAIRS - 1) as j:
            for u in range(3, UNITS):
                exps(u, j)
                copy_pT(u - 1, j)
            exps(0, j + 1)
            copy_pT(UNITS - 1, j)
            exps(1, j + 1)
            copy_pT(0, j + 1)
            exps(2, j + 1)
            oT_high(j)
            copy_pT(1, j + 1)
        for u in range(3, UNITS):
            exps(u, PAIRS - 1)
            copy_pT(u - 1, PAIRS - 1)
        def pool_high(g):
            act.wait_ge(pool_ps, g + 1)
            nc.scalar.activation(c_hi[:, PAIRS + g, :], bank[POOL_BANKS[g]][:], ACTF.Copy,
                                 scale=pool_sc16[:, g:g + 1]).then_inc(pool_hi, 1)

        for g in (0, 1):
            pool_high(g)
        copy_pT(UNITS - 1, PAIRS - 1)
        for g in (2, 3):
            pool_high(g)
        oT_high(PAIRS - 1)

        for b in range(FIRST_WOUT, FIRST_WQ - 1):
            hi(b + AHEAD)

        def ln_sqrt(tt, n):
            act.wait_ge(ln_var, n + 1)
            nc.scalar.activation(ln_rstd[:, tt, 0:1], ln_mv[:, tt, 1:2], ACTF.Sqrt,
                                 bias=eps_t[:]).then_inc(ln_std, 1)

        def normalize(r, tt, n, at=slice(0, D)):
            act.wait_ge(ln_scale, n + 1)
            nc.scalar.activation(r[:, tt, at], r[:, tt, at], ACTF.Identity, scale=ln_rstd[:, tt, 1:2],
                                 bias=ln_rstd[:, tt, 2:3]).then_inc(ln_norm, 1)

        def affine_T(tt):
            act.wait_ge(hT_ps, tt + 1)
            if tt >= 2:
                act.wait_ge(hT_lo, tt - 1)
            for c in range(KC):
                done = nc.scalar.activation(hT_f[:, tt % 2, c], hT_banks(tt)[c // 4][:, (c % 4) * P:(c % 4 + 1) * P],
                                            ACTF.Identity, scale=ln_gb16[:, 0, c:c + 1],
                                            bias=ln_gb16[:, 1, c:c + 1])
            done.then_inc(hT_affine, 1)

        for s in range(TT + 2):
            if s < TT:
                ln_sqrt(s, s)
            if 1 <= s <= TT:
                normalize(res, s - 1, s - 1)
            if s >= 2:
                affine_T(s - 2)
        hi(FIRST_WQ + 1)

        def query(hs, i=0):
            b = FIRST_WQ + hs
            hi(b + AHEAD, i)
            act.wait_ge(tile_used, num(b, i) + 1)
            if hs >= 2:
                act.wait_ge(sim_ps, num(hs, i) - 1)
            nc.scalar.activation(q_s[:, hs % 2], bank[b % 2][:], ACTF.Copy,
                                 scale=UNSCALE).then_inc(q_done, 1)
            if hs >= 1:
                copy_sim(hs - 1, i)

        def copy_sim(hs, i=0):
            act.wait_ge(sim_ps, num(hs, i) + 1)
            if hs >= 2:
                act.wait_ge(top_done, num(hs, i) - 1)
            nc.scalar.copy(sim[:, hs % 2].rearrange("p t k -> p (t k)"),
                           bank[5 + hs % 2][:]).then_inc(sim_sb, 1)

        for hs in range(Q_STRAIGHT):
            query(hs)
        with act.Fori(0, Q_LOOPS) as i:
            for k in range(STEP):
                query(Q_STRAIGHT + k, i)
        copy_sim(PEER_HEADS * SIDES - 1)

        act.wait_ge(res_out, 16)

        def gelu(m, i=0, later=False):
            b = FIRST_U + m
            act.wait_ge(tile_used, num(b, i) + 1)
            if m >= RAW or later:
                act.wait_ge(act_saved[m % RAW], 16 * (turn(m, i) - 1))
            nc.scalar.activation(act_out[:, m % RAW], bank[b % 2][:], ACTF.Gelu,
                                 scale=UNSCALE).then_inc(act_done, 1)

        def copy_w(tt, st, q):
            n = tt * (P // GROUP) + STEP_GROUPS * st + q
            act.wait_ge(wbank_done, n + RING + 1)
            nc.scalar.activation(w_buf[:, :, tt % 2, bass.ds(TOK_STEP * st + GROUP * q, GROUP)],
                                 w_bank[q % RING][:].rearrange("p (t i) -> p i t", t=GROUP), ACTF.Copy,
                                 scale=1.0 / GATE_SCALE).then_inc(wbank_free, 1)

        def gate_high(tt, st, q):
            act.wait_ge(eq_done, tt * (P // GROUP) + STEP_GROUPS * st + q + 1)
            for t in range(GROUP):
                c = GROUP * q + t
                done = nc.scalar.activation(oh1[:, q % RING, 0, t], eq1[:, q % RING, t], ACTF.Copy,
                                            scale=gate_cur[:, c:c + 1])
            done.then_inc(oh_hi_done, 1)

        def step(seg, st, later=False):
            for k in range(STEP):
                hi(FIRST_U + seg * SEG_TILES + k + AHEAD, st)
                if seg >= 1:
                    if k == 0:
                        act.wait_ge(pickT_done, seg)
                        nc.scalar.copy(gate_cur[:], pickT[:, 2, bass.ds(TOK_STEP * st, TOK_STEP)])
                        act.drain()
                    for q in GROUPS_AT[k]:
                        gate_high(seg - 1, st, q)
                gelu(seg * SEG_TILES + k, st, later)
                if seg >= 1:
                    for q in GROUPS_AT[k]:
                        copy_w(seg - 1, st, q)

        act.sem_inc(wbank_free, RING)
        for seg in range(N_SEG):
            if seg == 0:
                step(0, 0)
                with act.Fori(1, SEG_STEPS) as st:
                    step(0, st, True)
            else:
                if seg >= 3:
                    act.wait_ge(w_saved[seg - 3], 16 * 16)
                with act.Fori(0, SEG_STEPS) as st:
                    step(seg, st)
            if seg < N_SEG - 1:
                hi(FIRST_U + seg * SEG_TILES + SEG + AHEAD)
                act.wait_ge(score_done, seg + 1)
                nc.scalar.activation(score[:], score[:], ACTF.Exp).then_inc(exp_done, 1)
                gelu(seg * SEG_TILES + SEG)

        def g_high(m, i=0):
            act.wait_ge(g_done, num(m, i) + 1)
            if m >= 1:
                act.wait_ge(tile_used, num(FIRST_V + m, i) - SPLIT + 1)
            nc.scalar.activation(g_hi[:, m % SPLIT], g_f[:, m % SPLIT], ACTF.Copy,
                                 scale=ACT_SCALE).then_inc(g_hi_done, 1)

        for m in range(LAST_U, N_EXP):
            hi(FIRST_U + m + AHEAD)
            gelu(m)
            if m == N_EXP - 2:
                g_high(0)

        def v_body(m, i=0):
            if m + AHEAD < N_EXP:
                hi(FIRST_V + m + AHEAD, i)
            g_high(m + 1, i)

        with act.Fori(0, V_LOOPS) as i:
            for k in range(STEP):
                v_body(k, i)
        for m in range(V_LOOPS * STEP, N_EXP - 1):
            v_body(m)
        for s in range(TT):
            ln_sqrt(s, TT + s)
            if s >= 1:
                normalize(res2, s - 1, TT + s - 1)
        for half in range(2):
            normalize(res2, TT - 1, 2 * TT - 1, slice(half * T, (half + 1) * T))

    @block.vector
    def _(dve):
        def lo(b, i=0):
            dve.wait_ge(hi_done, num(b, i) + 1)
            nc.vector.scalar_tensor_tensor(
                out=w_lo[:, b % SPLIT], in0=raw[:, b % RAW], scalar=W_SCALE, in1=w_hi[:, b % SPLIT],
                op0=ALU.mult, op1=ALU.subtract).then_inc(lo_done, 1)

        def low_of(dst, src, high, scale=ACT_SCALE):
            return nc.vector.scalar_tensor_tensor(out=dst, in0=src, scalar=scale, in1=high,
                                                  op0=ALU.mult, op1=ALU.subtract)

        nc.vector.memset(eps_t[:], LN_EPS)
        for c in range(4):
            dve.wait_ge(x_hi_done, c + 1)
            low_of(a_lo[:, 2 * c:2 * c + 2], xT_t[:, 2 * c:2 * c + 2],
                   a_hi[:, 2 * c:2 * c + 2]).then_inc(x_lo_done, 1)
            if c < AHEAD:
                lo(c)
        def qk_low(b):
            name, ps = PROJ[b], bank[b % 2]
            dve.wait_ge(evac, b + 1)
            for g in range(GROUPS):
                rows, i = group_rows(g), QK.index(name)
                high, low = ((q_high(i - 2, g), q_two[rows, i - 2, 1] if g else q_moves[rows, i - 2])
                             if name[0] == "q" else (k_two[rows, i, g], k_low[rows, i, g]))
                done = low_of(low, ps[rows], high, QK_SCALE[name[0]])
            done.then_inc(low_evac, 1)

        for b in range(N_PROJ):
            lo(b + AHEAD)
            if b == 0:
                dve.wait_ge(frev_ps, 1)
                nc.vector.tensor_copy(frev[:, 0:FREV // 2], bank[5][0:HEADS, 0:FREV // 2])
                nc.vector.tensor_copy(frev[:, FREV // 2:], bank[6][0:HEADS, 0:FREV // 2]).then_inc(frev_sb, 1)
            if PROJ[b] in QK:
                qk_low(b)
            if b == 11:
                dve.wait_ge(kv_done, 1)
                low_of(kc_low[:].rearrange("p g n -> p (g n)"), bank[2][:, 0:GROUPS * N_CMP],
                       kc_two[:].rearrange("p g n -> p (g n)"), 1.0).then_inc(kc_done, 1)
            if b == 5:
                dve.wait_ge(wg_hi_done, 1)
                low_of(wg_lo, w_gates_t[:], wg_hi, W_SCALE).then_inc(wg_done, 1)
            if b == 6:
                dve.wait_ge(hid_ps, 1)
                nc.vector.tensor_copy(hid_pre[0:N_ROWS].rearrange("p a m -> p (a m)"),
                                      bank[2][0:N_ROWS, :]).then_inc(hid_pre_done, 1)
            if b == 7:
                dve.wait_ge(consts_in, 16 * 6)
                nc.vector.tensor_scalar(pool_sc16[:], pool_sc[:], ACT_SCALE, None, ALU.mult)
            if b == 9:
                gv = gates[:].rearrange("p t b h -> p (t b h)")
                dve.wait_ge(gates_exp, 1)
                nc.vector.tensor_scalar(gv, gv, 1.0, None, ALU.add)
                dve.drain()
                nc.vector.reciprocal(gv, gv)
                dve.drain()
                nc.vector.tensor_scalar(gates[:, 0, GATE_CMP], gates[:, 0, GATE_CMP], row_ok_t[:], None, ALU.mult)
                dve.drain()

        def bias_max(u, j):
            g, i, par = u // TT, u % TT, u % 2
            if i == 0:
                dve.wait_ge(bias_ready, GROUPS * j + g + 1)
            if not first_units(u, j):
                dve.wait_ge(e_done, branch(u - 2, j, WIN))
            first_c = T - (i + 1) * P
            for br in (SLC, WIN):
                dve.wait_ge(s_done, branch(u, j, br))
                dve.nop(nofuse=True)
                if i == 0 and br == WIN:
                    for c in range(TT):
                        c0 = T - (c + 1) * P + CMP_BLOCK - 1
                        nc.vector.tensor_tensor_reduce(
                            out=neg_xc[:, c, 0:n_cmp(c)], in0=bank[4][:, 32 * c:32 * c + n_cmp(c)],
                            in1=bias_cur[:, g, c0:c0 + CMP_STRIDE * (n_cmp(c) - 1) + 1:CMP_STRIDE],
                            scale=-1.0, scalar=HIGHEST, op0=ALU.add, op1=ALU.min,
                            accum_out=neg_max_c[:, c:c + 1])
                    dve.drain()
                    nc.vector.tensor_tensor(probs_c[:], neg_xc[:],
                                            neg_max_c[:].unsqueeze(2).to_broadcast([P, TT, 32]), ALU.subtract)
                nc.vector.tensor_tensor_reduce(
                    out=neg_x[:, par, br, 0:(i + 1) * P], in0=bank[2 * br + par][:, 0:(i + 1) * P],
                    in1=bias_cur[:, g, first_c:], scale=-1.0, scalar=HIGHEST,
                    op0=ALU.add, op1=ALU.min, accum_out=neg_max[:, par, br:br + 1]).then_inc(x_done, 1)

        def rescale(u, j):
            g, i, par = u // TT, u % TT, u % 2
            head = bass.ds(j + PAIRS * g, 1)
            dve.wait_ge(e_done, branch(u, j, WIN))
            dve.nop(nofuse=True)
            if i == 0:
                nc.vector.tensor_reduce(row_sum_c[:], probs_c[:], AX_X, ALU.add)
            nc.vector.reciprocal(row_scale[:, par, 0], row_sum[:, par])
            if i == 0:
                dve.drain()
                nc.vector.reciprocal(row_scale_c[:, 0], row_sum_c[:])
            dve.drain()
            if i == 0:
                nc.vector.tensor_tensor(row_scale_c[:, 1], row_scale_c[:, 0],
                                        gates[:, :, GATE_CMP, head].rearrange("p t o -> p (t o)"), ALU.mult)
            nc.vector.tensor_tensor(row_scale[:, par, 1], row_scale[:, par, 0],
                                    gates[:, i, GATE_CMP + 1:, head].rearrange("p b o -> p (b o)"),
                                    ALU.mult)
            dve.drain()
            if i == 0:
                nc.vector.tensor_tensor(probs_c[:], probs_c[:],
                                        row_scale_c[:, 1].unsqueeze(2).to_broadcast([P, TT, 32]), ALU.mult)
            n = (i + 1) * P
            for br in (SLC, WIN):
                nc.vector.tensor_scalar(probs[:, par, br, 0:n], probs[:, par, br, 0:n],
                                        row_scale[:, par, 1, br:br + 1], None, ALU.mult).then_inc(r_done, 1)

        nc.vector.memset(neg_xc[:], HIGHEST)
        dve.drain()
        dve.sem_inc(oT_free, 1)

        def unit(u, j):
            bias_max(u, j)
            rescale(u - 1, j)

        def oT_low(j):
            dve.wait_ge(oT_hi, j + 1)
            low_of(c_lo[:, j, :], bank[7][:], c_hi[:, j, :]).then_inc(oT_free, 1)

        bias_max(0, 0)
        unit(1, 0)
        unit(2, 0)
        with dve.Fori(0, PAIRS - 1) as j:
            for u in range(3, UNITS):
                unit(u, j)
            bias_max(0, j + 1)
            rescale(UNITS - 1, j)
            unit(1, j + 1)
            unit(2, j + 1)
            oT_low(j)
        for u in range(3, UNITS):
            unit(u, PAIRS - 1)
        rescale(UNITS - 1, PAIRS - 1)

        for g in range(POOL_GROUPS):
            dve.wait_ge(pool_hi, g + 1)
            low_of(c_lo[:, PAIRS + g, :], bank[POOL_BANKS[g]][:], c_hi[:, PAIRS + g, :],
                   pool_sc16[:, g:g + 1]).then_inc(pool_lo, 1)
        oT_low(PAIRS - 1)
        for b in range(FIRST_WOUT, FIRST_WQ - 1):
            lo(b + AHEAD)

        def ln_moments(r, tt, n, unscale):
            dve.wait_ge(mix_done, n + 1)
            for half, ps in enumerate(banks_of(tt)):
                h = slice(half * T, (half + 1) * T)
                nc.vector.scalar_tensor_tensor(out=r[:, tt, h], in0=ps[:], scalar=unscale, in1=r[:, tt, h],
                                               op0=ALU.mult, op1=ALU.add)
            dve.drain()
            for half in range(2):
                nc.vector.bn_stats(ln_stats[:, half], r[:, tt, half * T:(half + 1) * T])
            dve.drain()
            nc.vector.bn_aggr(ln_mv[:, tt], ln_stats[:].rearrange("p a b -> p (a b)")).then_inc(ln_var, 1)

        def ln_scales(tt, n):
            dve.wait_ge(ln_std, n + 1)
            nc.vector.reciprocal(ln_rstd[:, tt, 1:2], ln_rstd[:, tt, 0:1])
            dve.drain()
            nc.vector.scalar_tensor_tensor(out=ln_rstd[:, tt, 2:3], in0=ln_mv[:, tt, 0:1], scalar=-1.0,
                                           in1=ln_rstd[:, tt, 1:2], op0=ALU.mult,
                                           op1=ALU.mult).then_inc(ln_scale, 1)

        dve.wait_ge(res_ready, 1)
        nc.vector.tensor_scalar(ln_gb16[:], ln_gb[:], ACT_SCALE, None, ALU.mult)
        for s in range(TT + 3):
            if s < TT:
                ln_moments(res, s, s, UNSCALE)
            if 1 <= s <= TT:
                ln_scales(s - 1, s - 1)
            if s >= 3:
                tt = s - 3
                toks = slice(tt * P, (tt + 1) * P)
                dve.wait_ge(hT_affine, tt + 1)
                nc.vector.tensor_copy(a_hi[:, :, toks], hT_f[:, tt % 2])
                dve.drain()
                nc.vector.tensor_tensor(a_lo[:, :, toks], hT_f[:, tt % 2], a_hi[:, :, toks],
                                        ALU.subtract).then_inc(hT_lo, 1)
        lo(FIRST_WQ + 1)

        def top_keys(hs, i=0):
            s = sim[:, hs % 2]
            dve.wait_ge(sim_sb, num(hs, i) + 1)
            dve.nop(nofuse=True)
            for tt in range(TT):
                nc.vector.max(top_v[:, tt, 0:8], s[:, tt])
            dve.drain()
            for tt in range(TT):
                nc.vector.match_replace(sim_r[:, tt], in_to_replace=top_v[:, tt, 0:8], in_values=s[:, tt],
                                        imm_value=LOWEST)
            dve.drain()
            for tt in range(TT):
                nc.vector.max(top_v[:, tt, 8:16], sim_r[:, tt])
                nc.vector.max_index(top_i[:, tt, 0:8], top_v[:, tt, 0:8], s[:, tt])
            dve.drain()
            for tt in range(TT):
                nc.vector.max_index(top_i[:, tt, 8:16], top_v[:, tt, 8:16], sim_r[:, tt])
            dve.drain()
            head = hs // SIDES + (STEP // SIDES) * i
            for dst, src in ((picks_v, top_v), (picks_i, top_i)):
                done = nc.vector.tensor_copy(
                    dst[:, :, bass.ds(head, 1), hs % SIDES, :].rearrange("p t o k -> p t (o k)"), src)
            done.then_inc(top_done, 1)
            dve.drain()

        def query(hs, i=0):
            lo(FIRST_WQ + hs + AHEAD, i)
            if hs >= 1:
                top_keys(hs - 1, i)

        for hs in range(Q_STRAIGHT):
            query(hs)
        with dve.Fori(0, Q_LOOPS) as i:
            for k in range(STEP):
                query(Q_STRAIGHT + k, i)

        def best_pairs(tt, st, sub):
            h = bass.ds(2 * st + sub, 1)
            a = picks_v[:, tt, h, 0, :].rearrange("p o k -> p (o k)").unsqueeze(2).to_broadcast([P, TOPK, TOPK])
            b = picks_v[:, tt, h, 1, :].to_broadcast([P, TOPK, TOPK])
            nc.vector.tensor_tensor(cand, a, b, ALU.add)
            dve.drain()
            c, r = (t.rearrange("p a b -> p (a b)") for t in (cand, cand_r))
            nc.vector.max(best_v[:, 0:8], c)
            dve.drain()
            nc.vector.match_replace(r, in_to_replace=best_v[:, 0:8], in_values=c, imm_value=LOWEST)
            dve.drain()
            nc.vector.max(best_v[:, 8:16], r)
            nc.vector.max_index(best_i[:, 0:8], best_v[:, 0:8], c)
            dve.drain()
            nc.vector.max_index(best_i[:, 8:16], best_v[:, 8:16], r)
            nc.vector.tensor_scalar(score[:, h, :].rearrange("p o k -> p (o k)"), best_v[:], best_v[:, 0:1],
                                    None, ALU.subtract)
            dve.drain()

        def expert_ids(tt, st, sub):
            h = bass.ds(2 * st + sub, 1)
            nc.vector.tensor_scalar(best_ab[:, 0], best_i[:], 4, None, ALU.logical_shift_right)
            nc.vector.tensor_scalar(best_ab[:, 1], best_i[:], 15, None, ALU.bitwise_and)
            dve.drain()
            sides = [P, SIDES * TOPK, TOPK]
            nc.vector.tensor_tensor(eq[:].rearrange("p s k a -> p (s k) a"),
                                    best_ab[:].rearrange("p s k -> p (s k)").unsqueeze(2).to_broadcast(sides),
                                    iota16_t[:].unsqueeze(1).to_broadcast(sides), ALU.is_equal)
            dve.drain()
            ids = picks_i[:, tt, h].rearrange("p o s k -> p (o s) k").unsqueeze(2)
            nc.vector.tensor_tensor(eq[:], eq[:], ids.to_broadcast([P, SIDES, TOPK, TOPK]), ALU.mult)
            dve.drain()
            nc.vector.tensor_reduce(pick3[:, 0:2, h, :].rearrange("p s o k -> p s (o k)"), eq[:],
                                    AX_X, ALU.add)
            dve.drain()

        def one_hots(tt, st, q):
            dve.wait_ge(wbank_done, tt * (P // GROUP) + STEP_GROUPS * st + q + 1)
            for t in range(GROUP):
                c = GROUP * q + t
                nc.vector.tensor_scalar(eq1[:, q % RING, t], iota_t[:], pick_cur[:, 0, c:c + 1], None,
                                        ALU.is_equal)
                done = nc.vector.tensor_scalar(oh2[:, q % RING, t], iota_t[:], pick_cur[:, 1, c:c + 1], None,
                                               ALU.is_equal)
            done.then_inc(eq_done, 1)

        def step(seg, st, first=False):
            for k in range(STEP):
                if first:
                    lo(FIRST_U + k + AHEAD)
                if seg >= 1:
                    if k == 0:
                        dve.drain()
                        nc.vector.tensor_copy(pick_cur[:], pickT[:, 0:2, bass.ds(TOK_STEP * st, TOK_STEP)])
                        dve.drain()
                    for q in ROWS_AT[k]:
                        one_hots(seg - 1, st, q)
                if seg < TT:
                    if k == 1:
                        best_pairs(seg, st, 0)
                    if k == 3:
                        expert_ids(seg, st, 0)
                    if k == 5:
                        best_pairs(seg, st, 1)
                        expert_ids(seg, st, 1)
                if not first:
                    lo(FIRST_U + seg * SEG_TILES + k + AHEAD, st)
                elif k == 0:
                    top_keys(PEER_HEADS * SIDES - 1)

        dve.wait_ge(res_out, 16)
        for seg in range(N_SEG):
            if seg == 0:
                step(0, 0, first=True)
            with dve.Fori(int(seg == 0), SEG_STEPS) as st:
                step(seg, st)
            if seg < N_SEG - 1:
                dve.drain().then_inc(score_done, 1)
                lo(FIRST_U + seg * SEG_TILES + SEG + AHEAD)
                dve.wait_ge(exp_done, seg + 1)
                nc.vector.tensor_reduce(gsum[:, 0], score[:], AX_X, ALU.add)
                dve.drain()
                nc.vector.reciprocal(gsum[:, 1], gsum[:, 0])
                dve.drain()
                nc.vector.scalar_tensor_tensor(
                    out=pick3[:, 2], in0=score[:], scalar=GATE_SCALE,
                    in1=gsum[:, 1].unsqueeze(2).to_broadcast([P, PEER_HEADS, TOPK]),
                    op0=ALU.mult, op1=ALU.mult).then_inc(pick_done, 1)
                dve.wait_ge(pickT_ps, seg + 1)
                nc.vector.tensor_copy(pickT[:, 0:3].rearrange("p r t -> p (r t)"), bank[2][:, 0:3 * P])
                dve.drain()
                nc.vector.tensor_copy(gate_h[:], pickT[:, 2])
                dve.drain()
                nc.vector.tensor_tensor(pickT[:, 3], pickT[:, 2], gate_h[:], ALU.subtract)
                dve.drain().then_inc(pickT_done, 1)

        def g_product(m, i=0):
            s = m % RAW
            dve.wait_ge(act_back[s], 32 * turn(m, i))
            nc.vector.tensor_tensor(g_f[:, m % SPLIT, 0:2 * P], act_in[:, s, 0:2 * P], w_in_t[:, s], ALU.mult)
            nc.vector.tensor_tensor(
                g_f[:, m % SPLIT, 2 * P:].rearrange("p (b t) -> p b t", b=2),
                act_in[:, s, 2 * P:].rearrange("p (b t) -> p b t", b=2),
                w_buf[:, bass.ds(num(m, i), 1)].rearrange("p o b t -> p (o b) t"), ALU.mult).then_inc(g_done, 1)

        def g_low(m, i=0):
            dve.wait_ge(g_hi_done, num(m, i) + 1)
            low_of(g_lo[:, m % SPLIT], g_f[:, m % SPLIT], g_hi[:, m % SPLIT]).then_inc(g_lo_done, 1)

        def v_body(m, i=0):
            g_product(m + 1, i)
            if m + AHEAD < N_EXP:
                lo(FIRST_V + m + AHEAD, i)
            g_low(m + 1, i)

        for m in range(LAST_U, N_EXP):
            if m == N_EXP - 2:
                dve.wait_ge(wbank_free, RING + T // GROUP)
                g_product(0)
            lo(FIRST_U + m + AHEAD)
        g_low(0)
        with dve.Fori(0, V_LOOPS) as i:
            for k in range(STEP):
                v_body(k, i)
        for m in range(V_LOOPS * STEP, N_EXP - 1):
            v_body(m)
        dve.wait_ge(res_back, 16)
        dve.wait_ge(ln2_in, 32)
        for s in range(TT + 2):
            if s < TT:
                ln_moments(res2, s, TT + s, UNSCALE)
            if 1 <= s <= TT:
                ln_scales(s - 1, TT + s - 1)
            if s >= 2:
                tt = s - 2
                if tt < TT - 1:
                    dve.wait_ge(ln_norm, TT + tt + 1)
                    nc.vector.tensor_tensor(res2[:, tt], res2[:, tt], lng2[:], ALU.mult).then_inc(ln_gain, 1)
                    continue
                for half in range(2):
                    h = slice(half * T, (half + 1) * T)
                    dve.wait_ge(ln_norm, TT + tt + 1 + half)
                    nc.vector.tensor_tensor(res2[:, tt, h], res2[:, tt, h], lng2[:, h], ALU.mult)
                    dve.drain()
                    nc.vector.tensor_tensor(res2[:, tt, h], res2[:, tt, h], lnb2[:, h],
                                            ALU.add).then_inc(last_half, 1)

    @block.gpsimd
    def _(pool):
        nc.gpsimd.memset(zp[:, :, 0:PAD], 0.0)
        nc.gpsimd.memset(win[:, :, 0:PAD], 0.0)
        pool.drain()

        def copy_bias(g, j):
            nc.gpsimd.tensor_copy(bias_cur[:, g, :], bias_all[:, g, bass.ds(j, 1), :].rearrange("p o t -> p (o t)")
                                  if not isinstance(j, int) else bias_all[:, g, j, :])
            pool.drain().then_inc(bias_ready, 1)

        pool.wait_ge(bias_in, 16)
        for g in range(GROUPS):
            copy_bias(g, 0)

        with pool.Fori(0, PAIRS - 1) as j:
            for g in range(GROUPS):
                pool.wait_ge(x_done, branch(TT * (g + 1) - 1, j, WIN))
                copy_bias(g, j + 1)

        pool.wait_ge(inv_in, 16)
        pool.wait_ge(evac, N_PROJ)
        pool.drain()
        for g, window in enumerate(POOL_WINDOWS):
            src, shift, w = zp[:, g], 1, 0
            while shift < window:
                nc.gpsimd.tensor_tensor(win[:, w, PAD:], src[:, PAD:], src[:, PAD - shift:PAD + T - shift], ALU.add)
                pool.drain()
                src, w, shift = win[:, w], 1 - w, 2 * shift
            nc.gpsimd.tensor_tensor(win[:, w, PAD:], src[:, PAD:], inv_t[:, g], ALU.mult)
            pool.drain()
            nc.gpsimd.tensor_tensor(zp[:, g, PAD:], win[:, w, PAD:], zp[:, g, PAD:], ALU.subtract).then_inc(y_done, 1)
            pool.drain()

        pool.wait_ge(res_in, 16 * 4)
        for tt in range(TT):
            nc.gpsimd.tensor_scalar(res[:, tt], res[:, tt], ALPHA, 1.0, ALU.mult, ALU.mult)
            pool.drain()
        pool.sem_inc(res_ready, 1)

        for row in (lng, lnb):
            nc.gpsimd.tensor_scalar(row[:], row[:], ALPHA, 1.0, ALU.mult, ALU.mult)
            pool.drain()
        for tt in range(TT):
            pool.wait_ge(hT_ps, tt + 1)
            nc.gpsimd.tensor_tensor(res[:, tt], res[:, tt], lng[:], ALU.mult)
            pool.drain()
            nc.gpsimd.tensor_tensor(res[:, tt], res[:, tt], lnb[:], ALU.add)
            pool.drain().then_inc(res_alpha, 1)
        def gate_low(tt, st, q):
            pool.wait_ge(eq_done, tt * (P // GROUP) + STEP_GROUPS * st + q + 1)
            rest = pickT[:, 3, bass.ds(TOK_STEP * st + GROUP * q, GROUP)]
            nc.gpsimd.tensor_tensor(oh1[:, q % RING, 1], eq1[:, q % RING],
                                    rest.unsqueeze(2).to_broadcast([P, GROUP, P]), ALU.mult)
            pool.drain().then_inc(oh_lo_done, 1)

        for tt in range(TT):
            pool.wait_ge(pickT_done, tt + 1)
            with pool.Fori(0, SEG_STEPS) as st:
                for q in range(STEP_GROUPS):
                    gate_low(tt, st, q)

        pool.wait_ge(ln2_in, 32)
        for tt in range(TT - 1):
            pool.wait_ge(ln_gain, tt + 1)
            nc.gpsimd.tensor_tensor(res2[:, tt], res2[:, tt], lnb2[:], ALU.add)
            pool.drain().then_inc(ln_out, 1)

    @block.tensor
    def _(pe):
        mm = nc.tensor.matmul

        def three(ps, w_h, w_l, r_h, r_l, start, stop):
            mm(ps, w_h, r_h, start=start, stop=False)
            mm(ps, w_h, r_l, start=False, stop=False)
            return mm(ps, w_l, r_h, start=False, stop=stop)

        def wT_times_aT(b, i=0, x_waits=False):
            s, ps = b % SPLIT, bank[b % 2][:]
            pe.wait_ge(lo_done, num(b, i) + 1)
            for c in range(KC):
                if x_waits and c % 2 == 0:
                    pe.wait_ge(x_lo_done, c // 2 + 1)
                cols = slice(c * P, (c + 1) * P)
                done = three(ps, w_hi[:, s, cols], w_lo[:, s, cols], a_hi[:, c], a_lo[:, c],
                             c == 0, c == KC - 1)
            done.then_inc(tile_used, 1)

        def a_times_w(b):
            s = b % SPLIT
            pe.wait_ge(lo_done, b + 1)
            for tt in range(TT):
                for c in range(KC):
                    cols, toks = slice(c * P, (c + 1) * P), slice(tt * P, (tt + 1) * P)
                    done = three(bank[b % 2][:, toks], a_hi[:, c, toks], a_lo[:, c, toks],
                                 w_hi[:, s, cols], w_lo[:, s, cols], c == 0, c == KC - 1)
            done.then_inc(tile_used, 1)

        def rows_times_tile(b, i, tt, lhs_hi, lhs_lo, start=False, stop=False):
            s, toks = b % SPLIT, slice(tt * P, (tt + 1) * P)
            for lhs, rhs in ((lhs_hi, w_hi), (lhs_hi, w_lo), (lhs_lo, w_hi)):
                for half in range(2):
                    done = mm(banks_of(tt)[half][:], lhs[:, toks], rhs[:, s, half * T:(half + 1) * T],
                              start=start and lhs is lhs_hi and rhs is w_hi, stop=stop and lhs is lhs_lo)
            return done

        for b in range(N_PROJ):
            if b >= 2:
                pe.wait_ge(evac, b - 1)
                if PROJ[b - 2] in QK:
                    pe.wait_ge(low_evac, QK.index(PROJ[b - 2]) + 1)
            if PROJ[b] in ("vslc", "vwin"):
                a_times_w(b)
            else:
                wT_times_aT(b, x_waits=b == 0)
            if b == 0:
                pe.wait_ge(early_in, 16 * 3)
                for half in range(2):
                    done = mm(bank[5 + half][0:HEADS, 0:FREV // 2], rel_t[:],
                              onehot_t[:, half * (FREV // 2):(half + 1) * (FREV // 2)], start=True, stop=True)
                done.then_inc(frev_ps, 1)
            if b == 6:
                pe.wait_ge(cmp_w_in, 16 * 6)
                pe.wait_ge(wg_done, 1)
                for tt in range(TT):
                    for c in range(KC):
                        toks = slice(tt * P, (tt + 1) * P)
                        done = three(bank[4][:, tt * 3 * HEADS:(tt + 1) * 3 * HEADS], a_hi[:, c, toks],
                                     a_lo[:, c, toks], wg_hi[:, c], wg_lo[:, c], c == 0, c == KC - 1)
                done.then_inc(gates_ps, 1)
                pe.wait_ge(pe_in, 16)
                half_block = CMP_BLOCK // 2
                for kv in range(2):
                    for bb in range(half_block):
                        blocks = cmp_in[:, kv, bb:bb + CMP_STRIDE // 2 * (N_ROWS - 1) + 1:CMP_STRIDE // 2]
                        done = mm(bank[2][0:N_ROWS, kv * CMP_HIDDEN:(kv + 1) * CMP_HIDDEN], blocks,
                                  w1_t[:, kv, bb], start=bb == 0, stop=bb == half_block - 1)
                done.then_inc(hid_ps, 1)
            if b == 7:
                pe.wait_ge(hid_pre_done, 1)
                for kv in range(2):
                    for mh in range(2):
                        done = mm(hid_bank(kv, mh), hid_pre[0:N_ROWS, kv, mh * P:(mh + 1) * P],
                                  spread_t[:], start=True, stop=True)
                done.then_inc(hid_T, 1)
            if b == 9:
                pe.wait_ge(hid_done, 1)
                for mh in range(2):
                    mm(bank[2][:, 0:GROUPS * N_CMP], w2k_t[:, mh], hid[:, 0, mh].rearrange("p g n -> p (g n)"),
                       start=mh == 0, stop=mh == 1)
                for g in range(GROUPS):
                    for mh in range(2):
                        done = mm(bank[2][0:N_CMP, 64 + g * DH:64 + (g + 1) * DH], hid[:, 1, mh, g],
                                  w2v_t[:, mh], start=mh == 0, stop=mh == 1)
                done.then_inc(kv_ps, 1)

        pe.wait_ge(evac, N_PROJ)
        pe.wait_ge(kc_done, 1)
        pe.wait_ge(dup_done, 16 * (2 * PAIRS + 3 * 2))

        def scores(u, j):
            g, i, par = u // TT, u % TT, u % 2
            n = (i + 1) * P
            if not first_units(u, j):
                pe.wait_ge(x_done, branch(u - 2, j, WIN))

            def product(ps, toks, k_both, k_l):
                q = q_two[:, bass.ds(j, 1), g, toks].rearrange("p o t -> p (o t)")
                q_hi = q_two[0:DH, bass.ds(j, 1), g, toks].rearrange("p o t -> p (o t)")
                mm(ps, q, k_both, start=True, stop=False)
                return mm(ps, q_hi, k_l, start=False, stop=True)

            toks = slice(i * P, (i + 1) * P)
            product(bank[par][:, 0:n], toks, k_two[:, SLC, g, 0:n], k_low[0:DH, SLC, g, 0:n]).then_inc(s_done, 1)
            if i == 0:
                if not first_units(u, j):
                    pe.wait_ge(pt_cmp, GROUPS * j + g)
                for c in range(TT):
                    product(bank[4][:, 32 * c:32 * c + n_cmp(c)], slice(c * P, (c + 1) * P),
                            kc_two[:, g, 0:n_cmp(c)], kc_low[0:DH, g, 0:n_cmp(c)])
            product(bank[2 + par][:, 0:n], toks, k_two[:, WIN, g, 0:n], k_low[0:DH, WIN, g, 0:n]).then_inc(s_done, 1)

        def transposes(u, j):
            i, par = u % TT, u % 2
            for br, ps in ((SLC, bank[5]), (WIN, bank[6])):
                pe.wait_ge(r_done, branch(u, j, br))
                if u >= 1 or not first_units(u, j):
                    pe.wait_ge(pt_act, branch(u - 1, j, br))
                if i == 0 and br == SLC:
                    for c in range(TT):
                        nc.tensor.transpose(bank[4][0:N_CMP, c * P:(c + 1) * P], probs_c[:, c, 0:N_CMP],
                                            ident[:])
                for c in range(i + 1):
                    cols = slice(c * P, (c + 1) * P)
                    done = nc.tensor.transpose(ps[:, cols], probs[:, par, br, cols], ident[:])
                done.then_inc(t_done, 1)

        def outputs(u, j):
            g, i, par = u // TT, u % TT, u % 2
            cols = slice(g * DH, (g + 1) * DH)
            ps = bank[7][cols, i * P:(i + 1) * P]
            if u == 0:
                pe.wait_ge(oT_free, j + 1)
            if i == 0:
                pe.wait_ge(pt_cmp, GROUPS * j + g + 1)
            mm(ps, v_cmp[:, g, :], probsT_c[:, g, i * P:(i + 1) * P], start=True, stop=False)
            for v, br in ((v_slc, SLC), (v_win, WIN)):
                pe.wait_ge(pt_act, branch(u, j, br))
                for c in range(i + 1):
                    done = mm(ps, v[:, c, cols], probsT[:, par, br, c * P:(c + 1) * P], start=False,
                              stop=br == WIN and c == i)
            done.then_inc(pv_done, 1)

        def pool_product(g):
            ps = bank[POOL_BANKS[g]]
            pe.wait_ge(y_done, g + 1)
            pe.wait_ge(x_done, branch(UNITS - 2 + g // 2, PAIRS - 1, WIN))
            mm(ps[:], pool_wt[:, g], zp[:, g, PAD:], start=True, stop=True).then_inc(pool_ps, 1)

        def unit(u, j):
            if u < UNITS - 1:
                scores(u + 1, j)
            transposes(u - 1, j)
            outputs(u - 2, j)

        for u in range(3):
            scores(u, 0)
        transposes(0, 0)
        scores(3, 0)
        transposes(1, 0)
        outputs(0, 0)
        with pe.Fori(0, PAIRS - 1) as j:
            for u in range(3, UNITS - 1):
                unit(u, j)
            scores(0, j + 1)
            unit(UNITS - 1, j)
            scores(1, j + 1)
            transposes(UNITS - 1, j)
            outputs(UNITS - 2, j)
            scores(2, j + 1)
            transposes(0, j + 1)
            outputs(UNITS - 1, j)
            unit(2, j + 1)
        for u in range(3, UNITS - 1):
            unit(u, PAIRS - 1)
        pool_product(0)
        unit(UNITS - 1, PAIRS - 1)
        pool_product(1)
        transposes(UNITS - 1, PAIRS - 1)
        outputs(UNITS - 2, PAIRS - 1)
        pool_product(2)
        pool_product(3)
        outputs(UNITS - 1, PAIRS - 1)

        pe.wait_ge(pool_lo, POOL_GROUPS)
        for n, c in enumerate(WOUT_CHUNKS[:-2]):
            pe.wait_ge(lo_done, FIRST_WOUT + n + 1)
            for tt in range(TT):
                if n == 0 and tt == TT - 1:
                    pe.wait_ge(oT_free, PAIRS + 1)
                done = rows_times_tile(FIRST_WOUT + n, 0, tt, c_hi[:, c], c_lo[:, c], start=n == 0)
            done.then_inc(tile_used, 1)
        pe.wait_ge(lo_done, FIRST_WQ)
        for tt in range(TT):
            for n, c in ((KC - 2, WOUT_CHUNKS[-2]), (KC - 1, WOUT_CHUNKS[-1])):
                done = rows_times_tile(FIRST_WOUT + n, 0, tt, c_hi[:, c], c_lo[:, c], stop=n == KC - 1)
            done.then_inc(mix_done, 1)
        pe.drain().then_inc(tile_used, 2)

        for s in range(TT + 1):
            if s < TT:
                pe.wait_ge(ln_norm, s + 1)
                if s < TT - 1:
                    pe.wait_ge(ln_var, s + 2)
                else:
                    pe.wait_ge(hT_affine, 1)
                for c in range(KC):
                    done = nc.tensor.transpose(hT_banks(s)[c // 4][:, (c % 4) * P:(c % 4 + 1) * P],
                                               res[:, s, c * P:(c + 1) * P], ident[:])
                done.then_inc(hT_ps, 1)
            if s >= 1:
                toks = slice((s - 1) * P, s * P)
                pe.wait_ge(hT_lo, s)
                pe.wait_ge(lo_done, FIRST_WQ + 1)
                for c in range(KC):
                    cols, slot = slice(c * P, (c + 1) * P), FIRST_WQ % SPLIT
                    done = three(bank[FIRST_WQ % 2][:, toks], w_hi[:, slot, cols], w_lo[:, slot, cols],
                                 a_hi[:, c, toks], a_lo[:, c, toks], c == 0, c == KC - 1)
        done.then_inc(tile_used, 1)

        def similarities(hs, i=0):
            pe.wait_ge(q_done, num(hs, i) + 1)
            if hs >= 2:
                pe.wait_ge(sim_sb, num(hs, i) - 1)
            for tt in range(TT):
                toks = slice(tt * P, (tt + 1) * P)
                done = mm(bank[5 + hs % 2][:, toks], q_s[:, hs % 2, toks], subk_t[:, hs % SIDES],
                          start=True, stop=True)
            done.then_inc(sim_ps, 1)

        def query(hs, i=0):
            if hs >= 2:
                pe.wait_ge(q_done, num(hs, i) - 1)
            if hs >= 1:
                wT_times_aT(FIRST_WQ + hs, i)
            if hs >= 1:
                similarities(hs - 1, i)

        pe.wait_ge(subk_in, 16)
        for hs in range(Q_STRAIGHT):
            query(hs)
        with pe.Fori(0, Q_LOOPS) as i:
            for k in range(STEP):
                query(Q_STRAIGHT + k, i)
        similarities(PEER_HEADS * SIDES - 1)

        pe.sem_inc(wbank_done, RING)

        def experts(m, i=0, later=False):
            if m >= 2 or later:
                pe.wait_ge(act_done, num(m, i) - 1)
            else:
                pe.wait_ge(q_done, PEER_HEADS * SIDES - 1 + m)
            wT_times_aT(FIRST_U + m, i)

        def retrieval(tt, st, q):
            n = tt * (P // GROUP) + STEP_GROUPS * st + q
            pe.wait_ge(oh_hi_done, n + 1)
            pe.wait_ge(oh_lo_done, n + 1)
            pe.wait_ge(wbank_free, n + 1)
            for t in range(GROUP):
                ps = w_bank[q % RING][:, t * P:(t + 1) * P]
                mm(ps, oh2[:, q % RING, t], oh1[:, q % RING, 0, t], start=True, stop=False)
                done = mm(ps, oh2[:, q % RING, t], oh1[:, q % RING, 1, t], start=False, stop=True)
            done.then_inc(wbank_done, 1)

        def step(seg, st, later=False):
            for k in range(STEP):
                experts(seg * SEG_TILES + k, st, later)
                if seg >= 1:
                    for q in GROUPS_AT[k]:
                        retrieval(seg - 1, st, q)

        for seg in range(N_SEG):
            if seg == 0:
                step(0, 0)
                with pe.Fori(1, SEG_STEPS) as st:
                    step(0, st, True)
            else:
                with pe.Fori(0, SEG_STEPS) as st:
                    step(seg, st)
            if seg < N_SEG - 1:
                experts(seg * SEG_TILES + SEG)
                pe.wait_ge(pick_done, seg + 1)
                for row in range(3):
                    done = nc.tensor.transpose(bank[2][:, row * P:(row + 1) * P],
                                               pick3[:, row].rearrange("p h k -> p (h k)"), ident[:])
                done.then_inc(pickT_ps, 1)
        for m in range(LAST_U, N_EXP):
            experts(m)

        pe.wait_ge(wbank_free, RING + T // GROUP)

        def v_tile(m, i=0, start=False):
            pe.wait_ge(g_lo_done, num(m, i) + 1)
            pe.wait_ge(lo_done, num(FIRST_V + m, i) + 1)
            for tt in (1, 2, 3, 0) if start else range(TT):
                if start and tt == 0:
                    pe.wait_ge(act_done, N_EXP)
                done = rows_times_tile(FIRST_V + m, i, tt, g_hi[:, m % SPLIT], g_lo[:, m % SPLIT], start=start)
            done.then_inc(tile_used, 1)

        v_tile(0, start=True)
        with pe.Fori(0, V_LOOPS) as i:
            for k in range(STEP):
                v_tile(k + 1, i)
        for m in range(V_LOOPS * STEP + 1, N_EXP - SPLIT):
            v_tile(m)
        last, ready = range(N_EXP - SPLIT, N_EXP), set()
        for tt, m in [(0, last[0]), (1, last[0])] + [(tt, m) for tt in range(TT) for m in last
                                                     if tt > 1 or m > last[0]]:
            if m not in ready:
                pe.wait_ge(g_lo_done, m + 1)
                pe.wait_ge(lo_done, FIRST_V + m + 1)
                ready.add(m)
            done = rows_times_tile(FIRST_V + m, 0, tt, g_hi[:, m % SPLIT], g_lo[:, m % SPLIT],
                                   stop=m == N_EXP - 1)
            if m == N_EXP - 1:
                done.then_inc(mix_done, 1)

    return ctx


def _bucket(dist):
    d = np.maximum(dist, 0)
    exact = N_BUCKETS // 2
    f = np.float32
    big = exact + (np.log(np.maximum(d, 1).astype(f) / f(exact)) / f(np.log(MAX_DISTANCE / exact))
                   * f(N_BUCKETS - exact)).astype(np.int32)
    return np.where(d < exact, d, np.minimum(big, N_BUCKETS - 1))


def kernel(x, w_in, rel_table, cmp_pe_k, cmp_pe_v, cmp_k_w1, cmp_k_w2, cmp_v_w1, cmp_v_w2, pool_w,
           pool_scale, w_out, ln1_g, ln1_b, peer_wq, peer_subkeys, peer_u, peer_v, ln2_g, ln2_b):
    import concourse.bacc as bacc
    from concourse.bass_utils import run_bass_kernel_spmd

    x, w_in, w_out, wq, u, v = (np.asarray(a)[0] for a in (x, w_in, w_out, peer_wq, peer_u, peer_v))
    nsa, kv = HEADS * DH, GROUPS * DH
    names = ["kc", "vc", "kslc", "vslc", "kwin", "vwin"]
    at = {n: nsa + kv * i for i, n in enumerate(names)}
    gate0 = nsa + 6 * kv
    z0 = gate0 + 3 * HEADS
    cols = []
    for name in PROJ:
        if name[:2] in ("kc", "vc"):
            g = int(name[2])
            one = list(range(at[name[:2]] + g * DH, at[name[:2]] + (g + 1) * DH))
            cols += one + one
        elif name[0] == "q":
            j = int(name[1])
            cols += [h * DH + d for h in (j, j + PAIRS) for d in range(DH)]
        elif name[0] == "z":
            cols += list(range(z0 + int(name[1]) * P, z0 + (int(name[1]) + 1) * P))
        else:
            cols += list(range(at[name], at[name] + P))

    def column_tiles(w):
        return w.reshape(KC, P, -1, P).transpose(2, 1, 0, 3).reshape(-1, P, D)

    rows = []
    for c in WOUT_CHUNKS:
        if c < PAIRS:
            rows += [h * DH + d for h in (c, c + PAIRS) for d in range(DH)]
        else:
            rows += list(range(c * P, (c + 1) * P))
    stream = np.empty((N_TILES, P, D), np.float32)
    stream[:FIRST_WOUT] = column_tiles(w_in[:, cols])
    stream[FIRST_WOUT:FIRST_WQ] = w_out[rows].reshape(KC, P, D)
    stream[FIRST_WQ:FIRST_U] = column_tiles(wq)
    stream[FIRST_U:FIRST_V] = u.reshape(N_EXP, P, KC, P).transpose(0, 3, 2, 1).reshape(N_EXP, P, D)
    stream[FIRST_V:] = v.reshape(N_EXP, P, D)

    dist = T - 1 - np.arange(FREV)
    onehot = np.zeros((N_BUCKETS + 1, FREV), np.float32)
    onehot[_bucket(dist), np.arange(FREV)] = 1.0
    onehot[:, dist < 0] = 0.0
    onehot[N_BUCKETS, dist < 0] = 1.0
    counts = np.stack([1.0 / np.minimum(np.arange(T) + 1, w) for w in POOL_WINDOWS]).astype(np.float32)

    def every_row(a):
        return np.ascontiguousarray(np.broadcast_to(a, (P,) + a.shape))

    def pe_rows(a):
        return np.asarray(a)[0].reshape(CMP_BLOCK // 2, P).T

    spread = np.zeros((N_ROWS, GROUPS * N_CMP), np.float32)
    for g in range(GROUPS):
        spread[g * ROWS_OF_G:g * ROWS_OF_G + N_CMP, g * N_CMP:(g + 1) * N_CMP] = np.eye(N_CMP)
    spread[N_ROWS - 1] = 1.0
    w2k = np.asarray(cmp_k_w2)[0].reshape(2, P, DH).transpose(1, 0, 2)
    arrays = {
        "x": x[0] if x.ndim == 3 else x,
        "xT": (x[0] if x.ndim == 3 else x).T.reshape(KC, P, T).transpose(1, 0, 2),
        "stream": stream,
        "w_gates": w_in[:, gate0:z0].reshape(KC, P, 3 * HEADS).transpose(1, 0, 2),
        "rel": np.asarray(rel_table),
        "rel_neg": np.full((1, HEADS), NEG, np.float32),
        "onehot": onehot,
        "w1": np.stack([np.asarray(a)[0].reshape(CMP_BLOCK // 2, P, CMP_HIDDEN).transpose(1, 0, 2)
                        for a in (cmp_k_w1, cmp_v_w1)]),
        "w2k": np.concatenate([w2k, w2k], axis=2),
        "w2v": np.asarray(cmp_v_w2)[0].reshape(2, P, DH).transpose(1, 0, 2),
        "pe_kv": np.stack([pe_rows(cmp_pe_k), pe_rows(cmp_pe_v)], axis=1),
        "pool_w": np.asarray(pool_w)[0].transpose(1, 0, 2),
        "pool_scale": np.asarray(pool_scale)[0].reshape(POOL_GROUPS, P).T,
        "inv_cnt": every_row(counts),
        "row_ok": (np.arange(P) >= CMP_BLOCK - 1).astype(np.float32).reshape(P, 1),
        "ln1_g": every_row(np.asarray(ln1_g)[0]),
        "ln1_b": every_row(np.asarray(ln1_b)[0]),
        "ln1_gb": np.stack([np.asarray(a)[0].reshape(KC, P).T for a in (ln1_g, ln1_b)], axis=1),
        "subkeys": np.asarray(peer_subkeys)[0].transpose(2, 0, 1),
        "ln2_g": every_row(np.asarray(ln2_g)[0]),
        "ln2_b": every_row(np.asarray(ln2_b)[0]),
        "eye": np.eye(P, dtype=np.float32),
        "spread": spread,
        "iota_h": every_row(np.arange(P).astype(np.float16)),
        "iota16": every_row(np.arange(TOPK).astype(np.float32)),
    }
    nc = bacc.Bacc("TRN2", target_bir_lowering=False, num_devices=1)
    inputs, args = {}, []
    for name, a in arrays.items():
        a = np.ascontiguousarray(a)
        inputs[f"in_{name}"] = a
        args.append(nc.dram_tensor(f"in_{name}", a.shape, mybir.dt.from_np(a.dtype), kind="ExternalInput").ap())
    args.append(nc.dram_tensor("out", (T, D), F32, kind="ExternalOutput").ap())
    for name, shape in (("bias_rows", (HEADS, P, FREV)), ("gelu_act", (N_EXP, P, T)),
                        ("retrieval", (P, N_EXP, 2 * P)), ("residual", (T, D))):
        args.append(nc.dram_tensor(name, shape, F32, kind="Internal").ap())
    layer(nc, *args).close()
    r = run_bass_kernel_spmd(nc, [inputs], core_ids=[0])
    return r.results[0]["out"].reshape(1, T, D)
```
